# Optimizing a Trainium2 kernel written in Bass

```python
import jax, jax.numpy as jnp
from jax import lax
import numpy as np

D_MODEL = 1024
BATCH = 1
SEQ = 256
DEPTH = 2

CHUNK = 64
QBLOCK = 128
N_A_LAYERS = DEPTH // 2
N_B_LAYERS = DEPTH - N_A_LAYERS

GDN_HEAD_DIM = 128
GDN_HEADS = D_MODEL // GDN_HEAD_DIM
GDN_WIDTH = GDN_HEADS * GDN_HEAD_DIM
CONV_K = 4
GDN_PROJ = 4 * GDN_WIDTH + 2 * GDN_HEADS

MLA_HEADS = D_MODEL // 128
QK_NOPE = 128
QK_ROPE = 64
QK_HEAD = QK_NOPE + QK_ROPE
V_HEAD = 128
KV_LORA = D_MODEL // 4
Q_LORA = 3 * D_MODEL // 8
ROPE_BASE = 10000.0

D_FF = ((8 * D_MODEL // 3 + 127) // 128) * 128
N_MOD = 9
EPS = 1e-6
MAX_POS_OFFSET = 2048

kernel_name = "hybrid_gdn_mla_yoco_macaron_adaln"

def rms_norm(t, g):
    tf = t.astype(jnp.float32)
    y = tf * lax.rsqrt(jnp.mean(tf * tf, axis=-1, keepdims=True) + EPS)
    return (y * g.astype(jnp.float32)).astype(t.dtype)

def l2_norm(t):
    tf = t.astype(jnp.float32)
    return tf * lax.rsqrt(jnp.sum(tf * tf, axis=-1, keepdims=True) + EPS)

def modulate(t, g, shift, scale):
    return rms_norm(t, g) * (1 + scale[:, None, :]) + shift[:, None, :]

def swiglu(h, w_in, w_out):
    gate, up = jnp.split(h @ w_in, 2, axis=-1)
    return (jax.nn.silu(gate) * up) @ w_out

def rotary(t, positions):
    half = t.shape[-1] // 2
    inv_freq = ROPE_BASE ** (-jnp.arange(half, dtype=jnp.float32) / half)
    ang = positions.astype(jnp.float32)[..., None] * inv_freq
    cos = jnp.cos(ang)[:, :, None, :]
    sin = jnp.sin(ang)[:, :, None, :]
    tf = t.astype(jnp.float32)
    t1, t2 = tf[..., :half], tf[..., half:]
    return jnp.concatenate([t1 * cos - t2 * sin, t2 * cos + t1 * sin], axis=-1).astype(t.dtype)

def causal_depthwise_conv(t, w):
    k = w.shape[0]
    return lax.conv_general_dilated(
        t, w[:, None, :].astype(t.dtype), window_strides=(1,), padding=[(k - 1, 0)],
        dimension_numbers=("NWC", "WIO", "NWC"), feature_group_count=t.shape[-1])

def gated_delta_rule(q, k, v, g, beta):
    b_, s_, h_, dk = q.shape
    dv = v.shape[-1]
    nc = s_ // CHUNK
    q = q.astype(jnp.float32) * (dk ** -0.5)

    def to_chunks(t):
        return t.astype(jnp.float32).reshape(b_, nc, CHUNK, h_, -1).transpose(1, 0, 3, 2, 4)

    qc, kc, vc = to_chunks(q), to_chunks(k), to_chunks(v)
    gc = g.astype(jnp.float32).reshape(b_, nc, CHUNK, h_).transpose(1, 0, 3, 2)
    bc = beta.astype(jnp.float32).reshape(b_, nc, CHUNK, h_).transpose(1, 0, 3, 2)
    gcum = jnp.cumsum(gc, axis=-1)

    idx = jnp.arange(CHUNK)
    incl = idx[:, None] >= idx[None, :]
    strict = idx[:, None] > idx[None, :]
    diff = gcum[..., :, None] - gcum[..., None, :]
    decay = jnp.where(incl, jnp.exp(jnp.where(incl, diff, 0.0)), 0.0)

    kb = kc * bc[..., None]
    lower = jnp.where(strict, jnp.einsum("nbhid,nbhjd->nbhij", kb, kc) * decay, 0.0)
    eye = jnp.eye(CHUNK, dtype=jnp.float32)
    rhs = jnp.concatenate([vc * bc[..., None], kb * jnp.exp(gcum)[..., None]], axis=-1)
    sol = lax.linalg.triangular_solve(eye + lower, rhs, left_side=True, lower=True)
    u, w = sol[..., :dv], sol[..., dv:]
    attn_intra = jnp.where(incl, jnp.einsum("nbhid,nbhjd->nbhij", qc, kc) * decay, 0.0)

    def step(state, inp):
        qi, ki, ui, wi, gi, ai = inp
        v_new = ui - jnp.einsum("bhck,bhkv->bhcv", wi, state)
        o = jnp.einsum("bhck,bhkv->bhcv", qi * jnp.exp(gi)[..., None], state) \
            + jnp.einsum("bhcj,bhjv->bhcv", ai, v_new)
        g_last = gi[..., -1]
        k_dec = ki * jnp.exp(g_last[..., None] - gi)[..., None]
        state = state * jnp.exp(g_last)[..., None, None] + jnp.einsum("bhck,bhcv->bhkv", k_dec, v_new)
        return state, o

    state0 = jnp.zeros((b_, h_, dk, dv), jnp.float32)
    _, o = lax.scan(step, state0, (qc, kc, u, w, gcum, attn_intra))
    return o.transpose(1, 0, 3, 2, 4).reshape(b_, s_, h_, dv)

def gated_deltanet(h, w_in, conv_w, a_log, dt_bias, norm_g, w_out):
    b_, s_, _ = h.shape
    proj = h @ w_in
    qkv = proj[..., :3 * GDN_WIDTH]
    z = proj[..., 3 * GDN_WIDTH:4 * GDN_WIDTH]
    b_logit = proj[..., 4 * GDN_WIDTH:4 * GDN_WIDTH + GDN_HEADS]
    a_logit = proj[..., 4 * GDN_WIDTH + GDN_HEADS:]
    qkv = jax.nn.silu(causal_depthwise_conv(qkv, conv_w))
    q, k, v = [t.reshape(b_, s_, GDN_HEADS, GDN_HEAD_DIM) for t in jnp.split(qkv, 3, axis=-1)]
    q, k = l2_norm(q), l2_norm(k)
    beta = jax.nn.sigmoid(b_logit.astype(jnp.float32))
    g = -jnp.exp(a_log.astype(jnp.float32)) * jax.nn.softplus(
        a_logit.astype(jnp.float32) + dt_bias.astype(jnp.float32))
    o = gated_delta_rule(q, k, v, g, beta)
    zf = z.reshape(b_, s_, GDN_HEADS, GDN_HEAD_DIM).astype(jnp.float32)
    o = rms_norm(o, norm_g) * jax.nn.silu(zf)
    return o.reshape(b_, s_, GDN_WIDTH).astype(h.dtype) @ w_out

def mla_shared_kv(x, c, ada_w, ada_b, norm_g, w_dkv, kv_norm_g, w_ukv, k_norm_g, positions):
    b_, s_, _ = x.shape
    shift, scale = jnp.split(jax.nn.silu(c) @ ada_w + ada_b, 2, axis=-1)
    h = modulate(x, norm_g, shift, scale)
    ckv = h @ w_dkv
    latent = rms_norm(ckv[..., :KV_LORA], kv_norm_g)
    k_rope = ckv[..., KV_LORA:]
    kv = (latent @ w_ukv).reshape(b_, s_, MLA_HEADS, QK_NOPE + V_HEAD)
    k_nope, v = kv[..., :QK_NOPE], kv[..., QK_NOPE:]
    k = jnp.concatenate(
        [k_nope, jnp.broadcast_to(k_rope[:, :, None, :], (b_, s_, MLA_HEADS, QK_ROPE))], axis=-1)
    k = rms_norm(k, k_norm_g)
    k = jnp.concatenate([k[..., :QK_NOPE], rotary(k[..., QK_NOPE:], positions)], axis=-1)
    return k, v

def block_causal_attention(q, k, v):
    b_, s_, h_, dq = q.shape
    nqb = s_ // QBLOCK
    qb = q.reshape(b_, nqb, QBLOCK, h_, dq).transpose(1, 0, 2, 3, 4)
    key_chunk = jnp.arange(s_) // CHUNK
    scale = QK_HEAD ** -0.5

    def one_block(args):
        qi, blk = args
        s = jnp.einsum("bqhd,bkhd->bhqk", qi, k).astype(jnp.float32) * scale
        q_chunk = (blk * QBLOCK + jnp.arange(QBLOCK)) // CHUNK
        mask = key_chunk[None, :] <= q_chunk[:, None]
        s = jnp.where(mask, s, jnp.finfo(jnp.float32).min)
        p = jax.nn.softmax(s, axis=-1)
        return jnp.einsum("bhqk,bkhd->bqhd", p.astype(v.dtype), v)

    o = lax.map(one_block, (qb, jnp.arange(nqb)))
    return o.transpose(1, 0, 2, 3, 4).reshape(b_, s_, h_ * v.shape[-1])

def mla_attention(h, k, v, positions, w_dq, q_lora_norm_g, w_uq, q_norm_g, w_out):
    b_, s_, _ = h.shape
    q = rms_norm(h @ w_dq, q_lora_norm_g) @ w_uq
    q = rms_norm(q.reshape(b_, s_, MLA_HEADS, QK_HEAD), q_norm_g)
    q = jnp.concatenate([q[..., :QK_NOPE], rotary(q[..., QK_NOPE:], positions)], axis=-1)
    return block_causal_attention(q, k, v) @ w_out

def setup_inputs(seed: int = 0) -> dict:
    key = jax.random.key(seed)
    ks = iter(jax.random.split(key, 40))
    f32 = jnp.float32

    def nrm(shape, fan_in, scale=1.0):
        return jax.random.normal(next(ks), shape, f32) * (scale * fan_in ** -0.5)

    def gain(shape):
        return 1.0 + 0.02 * jax.random.normal(next(ks), shape, f32)

    def bias(shape):
        return 0.02 * jax.random.normal(next(ks), shape, f32)

    x = jax.random.normal(next(ks), (BATCH, SEQ, D_MODEL), f32)
    c = jax.random.normal(next(ks), (BATCH, D_MODEL), f32)
    offs = jax.random.randint(next(ks), (BATCH, 1), 0, MAX_POS_OFFSET)
    positions = (offs + jnp.arange(SEQ)[None, :]).astype(jnp.int32)

    dt = jnp.exp(jax.random.uniform(next(ks), (N_A_LAYERS, GDN_HEADS), f32,
                                    np.log(1e-3), np.log(1e-1)))
    return {
        "x": x,
        "c": c,
        "positions": positions,
        "ada_w": nrm((DEPTH, D_MODEL, N_MOD * D_MODEL), D_MODEL, 0.5),
        "ada_b": bias((DEPTH, N_MOD * D_MODEL)),
        "norm_g": gain((DEPTH, 3, D_MODEL)),
        "ffn_w_in": nrm((DEPTH, 2, D_MODEL, 2 * D_FF), D_MODEL),
        "ffn_w_out": nrm((DEPTH, 2, D_FF, D_MODEL), D_FF),
        "gdn_w_in": nrm((N_A_LAYERS, D_MODEL, GDN_PROJ), D_MODEL),
        "gdn_conv_w": nrm((N_A_LAYERS, CONV_K, 3 * GDN_WIDTH), CONV_K),
        "gdn_a_log": jnp.log(jax.random.uniform(next(ks), (N_A_LAYERS, GDN_HEADS), f32, 1.0, 16.0)),
        "gdn_dt_bias": dt + jnp.log(-jnp.expm1(-dt)),
        "gdn_norm_g": gain((N_A_LAYERS, GDN_HEAD_DIM)),
        "gdn_w_out": nrm((N_A_LAYERS, GDN_WIDTH, D_MODEL), GDN_WIDTH),
        "kv_ada_w": nrm((D_MODEL, 2 * D_MODEL), D_MODEL, 0.5),
        "kv_ada_b": bias((2 * D_MODEL,)),
        "kv_norm_g": gain((D_MODEL,)),
        "mla_w_dkv": nrm((D_MODEL, KV_LORA + QK_ROPE), D_MODEL),
        "mla_kv_norm_g": gain((KV_LORA,)),
        "mla_w_ukv": nrm((KV_LORA, MLA_HEADS * (QK_NOPE + V_HEAD)), KV_LORA),
        "mla_k_norm_g": gain((QK_HEAD,)),
        "mla_w_dq": nrm((N_B_LAYERS, D_MODEL, Q_LORA), D_MODEL),
        "mla_q_lora_norm_g": gain((N_B_LAYERS, Q_LORA)),
        "mla_w_uq": nrm((N_B_LAYERS, Q_LORA, MLA_HEADS * QK_HEAD), Q_LORA),
        "mla_q_norm_g": gain((N_B_LAYERS, QK_HEAD)),
        "mla_w_out": nrm((N_B_LAYERS, MLA_HEADS * V_HEAD, D_MODEL), MLA_HEADS * V_HEAD),
    }

def reference(x, c, positions, ada_w, ada_b, norm_g, ffn_w_in, ffn_w_out,
              gdn_w_in, gdn_conv_w, gdn_a_log, gdn_dt_bias, gdn_norm_g, gdn_w_out,
              kv_ada_w, kv_ada_b, kv_norm_g, mla_w_dkv, mla_kv_norm_g, mla_w_ukv, mla_k_norm_g,
              mla_w_dq, mla_q_lora_norm_g, mla_w_uq, mla_q_norm_g, mla_w_out):
    b_ = x.shape[0]
    c_act = jax.nn.silu(c)
    shared_k = shared_v = None
    for l in range(DEPTH):
        mod = (c_act @ ada_w[l] + ada_b[l]).reshape(b_, N_MOD, D_MODEL)
        h = modulate(x, norm_g[l, 0], mod[:, 0], mod[:, 1])
        x = x + 0.5 * mod[:, 2][:, None, :] * swiglu(h, ffn_w_in[l, 0], ffn_w_out[l, 0])
        h = modulate(x, norm_g[l, 1], mod[:, 3], mod[:, 4])
        if l < N_A_LAYERS:
            y = gated_deltanet(h, gdn_w_in[l], gdn_conv_w[l], gdn_a_log[l], gdn_dt_bias[l],
                               gdn_norm_g[l], gdn_w_out[l])
        else:
            j = l - N_A_LAYERS
            y = mla_attention(h, shared_k, shared_v, positions, mla_w_dq[j], mla_q_lora_norm_g[j],
                              mla_w_uq[j], mla_q_norm_g[j], mla_w_out[j])
        x = x + mod[:, 5][:, None, :] * y
        h = modulate(x, norm_g[l, 2], mod[:, 6], mod[:, 7])
        x = x + 0.5 * mod[:, 8][:, None, :] * swiglu(h, ffn_w_in[l, 1], ffn_w_out[l, 1])
        if l == N_A_LAYERS - 1:
            shared_k, shared_v = mla_shared_kv(x, c, kv_ada_w, kv_ada_b, kv_norm_g, mla_w_dkv,
                                               mla_kv_norm_g, mla_w_ukv, mla_k_norm_g, positions)
    return x


_drawn_inputs = setup_inputs


def setup_inputs(seed=0):
    import zlib

    import numpy as np

    out = dict(_drawn_inputs(seed))
    spreads = {}
    factors = {'norm_g': 6.269,
     'gdn_norm_g': 8.0,
     'kv_ada_b': 8.0,
     'kv_norm_g': 8.0,
     'mla_kv_norm_g': 23.992,
     'mla_k_norm_g': 8.0,
     'mla_q_lora_norm_g': 8.0,
     'mla_q_norm_g': 8.0}
    for name, (base, spread) in spreads.items():
        noise = np.random.default_rng([zlib.crc32(name.encode()), seed]).standard_normal(out[name].shape)
        drawn = base * np.exp(spread * noise) if base else spread * noise
        out[name] = __import__('jax').numpy.asarray(drawn.astype(out[name].dtype))
    for name, factor in factors.items():
        out[name] = (out[name] * factor).astype(out[name].dtype)
    return out
```

```python
from contextlib import ExitStack

import concourse.bass as bass
from concourse import mybir

F32 = mybir.dt.float32
F32R = mybir.dt.float32r
I32 = mybir.dt.int32
ALU = mybir.AluOpType
ACT = mybir.ActivationFunctionType
AX = mybir.AxisListType.X

P = 128
D = 1024
T = 256
KD = D // P
DFF = 2816
FT = DFF // P
HEADS = 8
EPS = 1e-6
TILES = 16
GW = TILES * P
RAW = 4
FFN_IN, FFN_OUT = FT, FT // 2
GDN_IN, PROJ_OUT = 16, 4
G_FFN = [0, 53, 90, 132]
G_GDN = 33
G_GDN_OUT = G_GDN + GDN_IN
G_KV = 86
G_MLA = 123
G_MLA_OUT = 128
GRANULES = 165
ADA_UNITS = 80
ADA_FIRST = 9
LEVELS = 7
KV_LORA_T, Q_LORA_T = 2, 3
QK_HEAD = 192
NEG = -1e30
TWO_PI = 6.283185307179586
RND = 12582912.0


def mod_index(layer, j):
    return j if layer == 0 else 11 + j


C_NORM = 0
C_KVN = 48
C_CONV = 56
C_GDNN = C_CONV + 96
C_KVL = C_GDNN + 1
C_QL = C_KVL + 2
C_KN = C_QL + 3
C_QN = C_KN + 2
C_FREQ = C_QN + 2
C_SIGN = C_FREQ + 1
C_COLS = C_SIGN + 1

M_ID, M_LE, M_GT, M_ST, M_LVT, M_SWAP, M_LOW, M_HIGH, M_LV = range(9)
M_COUNT = M_LV + LEVELS


def build(nc, x_in, c_in, pos, wstream, ada, ada_b, cols, tok, wba_dram, squares, out):
    ctx = ExitStack()
    with ctx:
        base = [nc.sbuf_base + (-nc.sbuf_base) % 64]

        def at(name, shape, dtype, offset):
            return nc.alloc_sbuf_tensor_at(name, shape, dtype, offset=offset)

        def sb(name, shape, dtype=F32):
            n = 4
            for s in shape[1:]:
                n *= s
            t = at(name, shape, dtype, base[0])
            base[0] += n + (-n) % 64
            return t

        def sem(name):
            return ctx.enter_context(nc.semaphore(name))

        bank = [ctx.enter_context(nc.psum_tensor(f"bank{i}", [P, 512], F32)) for i in range(8)]

        raw = sb("w_raw", [P, RAW, GW])
        wh = sb("w_hi", [P, 2, GW], F32R)
        wl = sb("w_lo", [P, 2, GW], F32R)
        araw = sb("ada_raw", [P, 2, KD, 256])
        acc = sb("ada_acc", [P, 256])
        x = sb("x", [P, KD, T])
        hh = sb("h_hi", [P, KD, T], F32R)
        hl = sb("h_lo", [P, KD, T], F32R)
        mods = sb("mods", [P, 2 * ADA_UNITS])
        modb = sb("mod_bias", [P, 2 * ADA_UNITS])
        col = sb("feature_consts", [P, C_COLS])
        mat = sb("square_consts", [P, M_COUNT, P])
        ones = sb("ones", [P, P])
        mean_d = sb("mean_d", [P, P])
        mean_hd = sb("mean_hd", [P, P])
        epsc = sb("eps_consts", [P, 4])
        craw = sb("c_raw", [P, KD])
        cact = sb("c_act", [P, KD])
        gs = sb("gain_scale", [P, KD])
        gate = sb("gate", [P, KD])
        warm = sb("warm", [P, 4])
        t2 = sb("norm_t", [P, 2, T])
        h32 = sb("norm_h", [P, 2, T])
        sq = sb("sq", [P, 2, 2 * T])
        std = sb("std", [P, 2, 2 * T])
        rstd = sb("rstd", [P, T])
        silu = sb("ff_silu_out", [P, 2, T])
        hid = sb("ff_hid32", [P, 2, T])
        cs = sb("cos_sin", [P, 2, T])
        shared = base[0]
        kn = sb("k_nope", [P, HEADS, T])
        kr = sb("k_rope", [P, HEADS // 2, T])
        vt = sb("v_tok", [P, 2, D])
        arena = base[0]
        fh = sb("ff_hid_hi", [P, FT, T], F32R)
        fl = sb("ff_hid_lo", [P, FT, T], F32R)
        ends = [base[0]]

        base[0] = shared
        KDC = sb("k_dec", [P, 512])
        RK = sb("rhs_k", [P, 512])
        SS = at("state", [P, 512], F32, base[0] - 2048)
        QG = sb("q_g", [P, 512])
        WT = sb("w_t", [P, 512])
        TMP = sb("masked_cols", [P, 2, 512])
        AT = sb("attn_t", [P, 2, 512])
        LT = sb("lower_t", [P, 2, 512])
        assert base[0] <= arena
        base[0] = arena
        qkv = sb("qkv", [P, 24, T])
        zs = sb("z_silu", [P, HEADS, T])
        wba = sb("wba", [P, KD, 16])
        wbah = sb("wba_hi", [P, KD, 16], F32R)
        wbal = sb("wba_lo", [P, KD, 16], F32R)
        tokc = sb("tok_consts", [P, 16])
        sc = sb("gate_scalars", [P, 14, 2, 8])
        X = sb("inv", [P, 2, 512])
        O32 = at("o32", [P, 4, T], F32, base[0] - 4096)
        XT = sb("inv_t", [P, 2, 512])
        BS = at("beta_strict", [P, 2, 512], F32, base[0] - 4096)
        PS = sb("inv_p", [P, 2, 512])
        DC = at("decay_t", [P, 2, 512], F32, base[0] - 4096)
        RV = sb("rhs_v", [P, 2, 512])
        U = at("u", [P, 2, 512], F32, base[0] - 4096)
        ends.append(base[0])

        base[0] = arena
        lat = sb("lat", [P, 3, T])
        lath = sb("lat_hi", [P, 3, T], F32R)
        latl = sb("lat_lo", [P, 3, T], F32R)
        qn = sb("q_nope", [P, HEADS, T])
        qr = sb("q_rope", [P, HEADS // 2, T])
        rot = sb("rot_t", [P, 2 * T])
        sqr = sb("rope_sq", [P, HEADS // 2, T])
        angi = sb("positions", [P, T], I32)
        ang = sb("angles", [P, 6, T])
        prb = sb("probs", [P, 2, 384])
        pt = sb("probs_t", [P, 2, 384])
        st = sb("soft_stats", [P, 2, 8])
        ends.append(base[0])
        assert max(ends) <= nc.sbuf_usable_end, (ends, nc.sbuf_usable_end)

        w_landed = [sem(f"w_landed{i}") for i in range(RAW)]
        w_hi, w_lo, w_used = sem("w_hi"), sem("w_lo"), sem("w_used")
        ada_landed = [sem(f"ada_landed{i}") for i in range(2)]
        ada_mac, ada_red, ada_done = sem("ada_mac"), sem("ada_red"), sem("ada_done")
        consts_in, x_in_sem, set_consts = sem("consts_in"), sem("x_in"), sem("set_consts")
        c_ready = sem("c_ready")
        x_upd, y_done = sem("x_upd"), sem("y_done")
        sq_ready, ss_mm, std_ready = sem("sq_ready"), sem("ss_mm"), sem("std_ready")
        mod_t, hh_ready, h_ready = sem("mod_t"), sem("hh_ready"), sem("h_ready")
        ff_silu, ff_hid, ff_hi, ff_lo = sem("ff_silu"), sem("ff_hid"), sem("ff_hi"), sem("ff_lo")
        gc_first, gc_tap, gc_conv, gc_silu, gz_silu = (sem("gc_" + n) for n in ("first", "tap", "conv", "silu", "z"))
        ba_in, ba_hi, ba_lo, ba_done = sem("ba_in"), sem("ba_hi"), sem("ba_lo"), sem("ba_done")
        dve_link, act_link = sem("dve_link"), sem("act_link")
        gt_act, gt_dve, gt_pe = sem("gt_act"), sem("gt_dve"), sem("gt_pe")
        l2_sq, l2_ss, l2_std, l2_done = (sem("l2_" + n) for n in ("sq", "ss", "std", "done"))
        co = {n: sem("co_" + n) for n in (
            "gm", "kq", "bs", "dd", "decay", "lt", "turned", "tokd", "u", "uu", "state", "state_sb", "ws", "vnew",
            "o0", "o1", "osb", "osq", "oss", "ostd", "onorm", "ohi", "olo")}
        inv_x = [sem(f"inv_x{b}") for b in range(2)]
        inv_p = [sem(f"inv_p{b}") for b in range(2)]
        inv_ps = [sem(f"inv_ps{b}") for b in range(2)]
        inv_xp = [sem(f"inv_xp{b}") for b in range(2)]
        am = {n: sem("am_" + n) for n in (
            "angle", "sin", "lev", "latsq", "latss", "latstd", "latn", "lathi", "latlo", "kraw", "kev", "qraw", "qev",
            "vev", "gained", "swap", "rot", "ropesq", "hsq", "hss", "hstd", "hn", "s", "max", "exp", "p", "turned",
            "pt", "o", "ohi", "olo")}
        pos_in = sem("pos_in_sem")
        stored = sem("stored")

        out_stages = {"ffn0": 0, "gdn": 1, "ffn1": 2, "ffn2": 3, "mla": 4, "ffn3": 5}
        last_v = len(out_stages) - 1
        granules, units = GRANULES, ADA_UNITS

        def half(b, e):
            return bank[b][:, e * T:(e + 1) * T]

        def wide(ap, n):
            return ap.unsqueeze(1).to_broadcast([P, n, ap.shape[-1]])

        def swap_bank(n, c):
            return bank[2][:, T:2 * T] if n == 1 else bank[4 + c][:, :]

        def heads4(ap):
            return ap.rearrange("p (h t) -> p h t", h=4)

        block = ctx.enter_context(nc.Block())

        @block.sync
        def _(sp):
            sp.dma_start(craw[:, :], c_in).then_inc(consts_in, 16)
            sp.dma_start(col[:, :], cols).then_inc(consts_in, 16)
            sp.dma_start(modb[:, :], ada_b).then_inc(consts_in, 16)
            sp.dma_start(x[:, :, :], x_in).then_inc(x_in_sem, 16)
            sp.dma_start(angi[:, :], pos).then_inc(pos_in, 16)
            sp.dma_start(mat[:, :, :], squares).then_inc(consts_in, 16)
            for g in range(RAW):
                sp.dma_start(raw[:, g, :], wstream[g]).then_inc(w_landed[g], 16)
            turns = (granules - RAW) // RAW
            with sp.Fori(0, turns) as i:
                for r in range(RAW):
                    sp.wait_ge(w_lo, i * RAW + (r + 1))
                    sp.dma_start(raw[:, r, :], wstream[i * RAW + (RAW + r)]).then_inc(w_landed[r], 16)
            for g in range(RAW + turns * RAW, granules):
                sp.wait_ge(w_lo, g - RAW + 1)
                sp.dma_start(raw[:, g % RAW, :], wstream[g]).then_inc(w_landed[g % RAW], 16)
            for m in range(KD):
                sp.wait_ge(x_upd, 8 * last_v + m + 1)
                sp.dma_start(out[:, m, :], x[:, m, :]).then_inc(stored, 16)
            sp.wait_ge(stored, 16 * KD)

        @block.gpsimd
        def _(pool):
            for u in range(2):
                pool.dma_start(araw[:, u, :, :], ada[u]).then_inc(ada_landed[u], 16)
            nc.gpsimd.memset(ones[:, :], 1.0)
            nc.gpsimd.memset(mean_d[:, :], 1.0 / D)
            nc.gpsimd.memset(mean_hd[:, :], 1.0 / P)
            nc.gpsimd.memset(epsc[:, 0:1], EPS)
            nc.gpsimd.memset(epsc[:, 1:2], EPS * P)
            nc.gpsimd.memset(epsc[:, 2:3], EPS * QK_HEAD)
            nc.gpsimd.memset(epsc[:, 3:4], 1.0).then_inc(set_consts, 1)
            with pool.Fori(0, units // 2 - 1) as i:
                for u in range(2):
                    pool.wait_ge(ada_mac, i * (2 * KD) + (u + 1) * KD)
                    pool.dma_start(araw[:, u, :, :], ada[i * 2 + (2 + u)]).then_inc(ada_landed[u], 16)

        @block.scalar
        def _(act):
            A = nc.scalar.activation

            def split_hi(g, r, at_start=False):
                act.wait_ge(w_landed[r], (g - r) * 4 + 16)
                if not at_start:
                    act.wait_ge(w_used, g - 1)
                nc.scalar.copy(wh[:, r % 2, :], raw[:, r, :]).then_inc(w_hi, 1)

            def split_next(g, r):
                if isinstance(g, int) and g + 2 >= granules:
                    return
                split_hi(g + 2, (r + 2) % RAW)

            def linked(n, ins):
                ins.then_inc(act_link, 1)
                act.wait_ge(act_link, n)

            def stats(v):
                for m in range(KD):
                    if v:
                        act.wait_ge(x_upd, 8 * (v - 1) + m + 1)
                    elif m == 0:
                        act.wait_ge(x_in_sem, 16)
                    if 8 * v + m >= 2:
                        act.wait_ge(ss_mm, 8 * v + m - 1)
                    A(sq[:, m % 2, 0:T], x[:, m, :], ACT.Square).then_inc(sq_ready, 1)
                    if m == KD - 2:
                        A(warm[:, 0:1], epsc[:, 3:4], ACT.Sqrt)
                act.wait_ge(ss_mm, 8 * v + KD)
                A(std[:, 0, 0:T], half(2, 0), ACT.Sqrt, bias=epsc[:, 0:1]).then_inc(std_ready, 1)

            def modulate(n, vec):
                if n == 4:
                    act.wait_ge(w_used, G_KV + 2)
                for m in range(KD):
                    act.wait_ge(mod_t, 8 * n + m + 1)
                    if 8 * n + m >= 2:
                        act.wait_ge(h_ready, 8 * n + m - 1)
                    s = 8 * vec + m
                    A(h32[:, m % 2, :], t2[:, m % 2, :], ACT.Identity, bias=mods[:, s:s + 1], scale=gs[:, m:m + 1])
                    A(hh[:, m, :], t2[:, m % 2, :], ACT.Identity, bias=mods[:, s:s + 1],
                      scale=gs[:, m:m + 1]).then_inc(hh_ready, 1)

            def ffn_in_step(f, g, j, r, par):
                act.wait_ge(w_used, g + 1)
                A(silu[:, par, :], half(par, 0), ACT.Silu).then_inc(ff_silu, 1)
                split_next(g, r)
                act.wait_ge(ff_hid, j + (22 * f + 1))
                nc.scalar.copy(fh[:, j, :], hid[:, par, :]).then_inc(ff_hi, 1)

            def ffn(f):
                g0 = G_FFN[f]
                for j in (0, 1):
                    ffn_in_step(f, g0 + j, j, (g0 + j) % RAW, j)
                with act.Fori(0, 5) as i:
                    for q in range(4):
                        ffn_in_step(f, i * 4 + (g0 + 2 + q), i * 4 + (2 + q), (g0 + 2 + q) % RAW, q % 2)
                g1 = g0 + FFN_IN
                turns = 1 if g1 + FFN_OUT == granules else 2
                split_next(g1, g1 % RAW)
                with act.Fori(0, turns) as i:
                    for q in range(4):
                        split_next(i * 4 + (g1 + 1 + q), (g1 + 1 + q) % RAW)
                for o in range(1 + 4 * turns, FFN_OUT):
                    split_next(g1 + o, (g1 + o) % RAW)

            def gdn():
                act.dma_start(wba[:, :, :], wba_dram).then_inc(ba_in, 16)
                act.dma_start(tokc[:, :], tok).then_inc(ba_in, 16)
                act.wait_ge(ba_in, 32)
                nc.scalar.copy(wbah[:, :, :], wba[:, :, :]).then_inc(ba_hi, 1)

                def tile_pair(g, r, n, t0, par):
                    act.wait_ge(w_used, g + 1)
                    for e in range(2):
                        act.wait_ge(gc_silu, t0 + (e - 1))
                        A(silu[:, e, :], half(par, e), ACT.Identity,
                          scale=col[:, bass.ds(t0 + (C_CONV + 72 + e), 1)]).then_inc(gc_first, 1)
                    split_next(g, r)
                    for e in range(2):
                        act.wait_ge(gc_conv, t0 + (e + 1))
                        A(qkv[:, t0 + e, :], silu[:, e, :], ACT.Silu).then_inc(gc_silu, 1)

                def first_pair():
                    g = G_GDN
                    act.wait_ge(w_used, g + 1)
                    for e in range(2):
                        A(silu[:, e, :], half(0, e), ACT.Identity,
                          scale=col[:, C_CONV + 72 + e:C_CONV + 73 + e]).then_inc(gc_first, 1)
                    split_next(g, g % RAW)
                    for e in range(2):
                        act.wait_ge(gc_conv, e + 1)
                        A(qkv[:, e, :], silu[:, e, :], ACT.Silu).then_inc(gc_silu, 1)

                first_pair()
                for n in range(1, 4):
                    tile_pair(G_GDN + n, (G_GDN + n) % RAW, n, 2 * n, n % 2)
                with act.Fori(0, 2) as i:
                    for n in range(4, 8):
                        tile_pair(i * 4 + (G_GDN + n), (G_GDN + n) % RAW, n, i * 8 + 2 * n, n % 2)
                act.wait_ge(gt_dve, 1)
                linked(1, A(sc[:, 9, :, :], sc[:, 6, :, :], ACT.Abs))
                A(sc[:, 8, :, :], sc[:, 7, :, :], ACT.Exp, scale=-1.0)
                linked(2, A(sc[:, 10, :, :], sc[:, 9, :, :], ACT.Exp, scale=-1.0))
                A(sc[:, 12, 0, :], tokc[:, 8:16], ACT.Exp)
                A(sc[:, 11, :, :], sc[:, 10, :, :], ACT.Ln, bias=epsc[:, 3:4]).then_inc(gt_act, 1)
                for n in range(12, 16):
                    g = G_GDN + n
                    act.wait_ge(w_used, g + 1)
                    z0 = 2 * (n - 12)
                    A(zs[:, z0:z0 + 2, :], bank[n % 2][:, :].rearrange("p (e t) -> p e t", e=2), ACT.Silu).then_inc(gz_silu, 1)
                    split_next(g, g % RAW)
                act.wait_ge(gt_pe, 1)
                A(sc[:, 3, :, :], bank[2][:, 32:48].rearrange("p (b h) -> p b h", b=2), ACT.Exp)
                A(sc[:, 4, :, :], bank[2][:, 48:64].rearrange("p (b h) -> p b h", b=2), ACT.Exp).then_inc(gt_act, 1)
                for p in range(8):
                    if p >= 2:
                        act.wait_ge(l2_ss, p - 1)
                    A(sq[:, p % 2, :].rearrange("p (e t) -> p e t", e=2), qkv[:, 2 * p:2 * p + 2, :], ACT.Square).then_inc(l2_sq, 1)
                    if p >= 1:
                        root(p - 1)
                root(7)
                for hg in range(2):
                    for b in range(2):
                        s = 2 * hg + b
                        act.wait_ge(co["dd"], s + 1)
                        A(DC[:, b, :], DC[:, b, :], ACT.Exp)
                        if b:
                            A(QG[:, :], bank[6 + b][:, :], ACT.Exp)
                        A(warm[:, 2:3], epsc[:, 3:4], ACT.Copy).then_inc(co["decay"], 1)
                        act.wait_ge(co["decay"], s + 1)
                    for b in range(2):
                        act.wait_ge(co["o0" if b == 0 else "o1"], hg + 1)
                        A(O32[:, :, b * P:(b + 1) * P], heads4(bank[(4, 1)[b]][:, :]), ACT.Copy).then_inc(co["osb"], 1)
                    act.wait_ge(co["osb"], 2 * hg + 2)
                    for p in range(2):
                        q = 2 * hg + p
                        A(sq[:, p, :].rearrange("p (e t) -> p e t", e=2), O32[:, 2 * p:2 * p + 2, :], ACT.Square).then_inc(co["osq"], 1)
                    for p in range(2):
                        q = 2 * hg + p
                        act.wait_ge(co["oss"], q + 1)
                        A(std[:, p, :], bank[p and 6][:, :], ACT.Sqrt, bias=epsc[:, 0:1]).then_inc(co["ostd"], 1)
                    for p in range(2):
                        q = 2 * hg + p
                        act.wait_ge(co["onorm"], q + 1)
                        A(hh[:, 2 * q:2 * q + 2, :], O32[:, 2 * p:2 * p + 2, :], ACT.Copy).then_inc(co["ohi"], 1)
                for g in range(G_GDN_OUT, G_GDN_OUT + PROJ_OUT):
                    split_next(g, g % RAW)

            def root(p):
                act.wait_ge(l2_ss, p + 1)
                if p >= 2:
                    act.wait_ge(l2_done, p - 1)
                q = p < 4
                A(std[:, p % 2, :], bank[p % 2][:, :], ACT.Sqrt, bias=epsc[:, 1:2] if q else epsc[:, 0:1],
                  scale=float(P) if q else 1.0).then_inc(l2_std, 1)

            def latent(nt, first, root_scale):
                act.wait_ge(am["latss"], 1 if first else 2)
                A(std[:, 0, 0:T], half(2, 0), ACT.Sqrt, bias=epsc[:, 0:1], scale=root_scale).then_inc(am["latstd"], 1)
                c0, i0 = (C_KVL, 0) if first else (C_QL, 2)
                for i in range(nt):
                    act.wait_ge(am["latn"], i0 + i + 1)
                    if i0 + i >= 2:
                        act.wait_ge(am["latlo"], i0 + i - 1)
                    A(h32[:, i % 2, :], lat[:, i, :], ACT.Identity, scale=col[:, c0 + i:c0 + i + 1])
                    A(lath[:, i, :], lat[:, i, :], ACT.Identity, scale=col[:, c0 + i:c0 + i + 1]).then_inc(am["lathi"], 1)

            def head_norms(nope, first):
                p0 = 0 if first else 4
                for j in range(4):
                    p = p0 + j
                    if p >= 2:
                        act.wait_ge(am["hss"], p - 1)
                    A(sq[:, j % 2, :].rearrange("p (e t) -> p e t", e=2), nope[:, 2 * j:2 * j + 2, :], ACT.Square).then_inc(am["hsq"], 1)
                    if j:
                        head_root(p - 1, first)
                head_root(p0 + 3, first)

            def head_root(p, first):
                act.wait_ge(am["hss"], p + 1)
                if p >= 2:
                    act.wait_ge(am["hn"], p - 1)
                A(std[:, p % 2, :], bank[p % 2][:, :], ACT.Sqrt, bias=epsc[:, 0:1] if first else epsc[:, 2:3],
                  scale=1.0 / QK_HEAD if first else 1.0).then_inc(am["hstd"], 1)

            def kv():
                g = G_KV
                act.wait_ge(w_used, g + 1)
                A(lat[:, 0:2, :], bank[0][:, :].rearrange("p (e t) -> p e t", e=2), ACT.Copy)
                A(sq[:, 0, :], bank[0][:, :], ACT.Square).then_inc(am["latsq"], 1)
                split_next(g, g % RAW)
                act.wait_ge(w_used, g + 2)
                A(lat[:, 2, :], half(1, 0), ACT.Copy).then_inc(am["lev"], 1)
                A(sqr[:, 0, :], half(1, 0), ACT.Square).then_inc(am["ropesq"], 1)
                split_next(g + 1, (g + 1) % RAW)
                latent(KV_LORA_T, True, 1.0 / (KV_LORA_T * P))
                for p in range(4):
                    if p < 3:
                        act.wait_ge(am["kraw"], p + 1)
                    else:
                        act.wait_ge(w_used, g + 3)
                    A(kn[:, 2 * p:2 * p + 2, :], bank[p % 2][:, :].rearrange("p (e t) -> p e t", e=2), ACT.Copy).then_inc(am["kev"], 1)
                split_next(g + 2, (g + 2) % RAW)
                act.wait_ge(w_used, g + 4)
                for b in range(2):
                    for c in range(2):
                        A(vt[:, b, 512 * c:512 * c + 512], bank[4 + 2 * b + c][:, :], ACT.Copy).then_inc(am["vev"], 1)
                split_next(g + 3, (g + 3) % RAW)
                head_norms(kn, True)

            def mla():
                g = G_MLA
                act.wait_ge(w_used, g + 1)
                A(lat[:, 0:2, :], bank[0][:, :].rearrange("p (e t) -> p e t", e=2), ACT.Copy)
                A(sq[:, 0, :], bank[0][:, :], ACT.Square).then_inc(am["latsq"], 1)
                split_next(g, g % RAW)
                act.wait_ge(w_used, g + 2)
                A(lat[:, 2, :], half(1, 0), ACT.Copy).then_inc(am["lev"], 1)
                A(sq[:, 1, 0:T], half(1, 0), ACT.Square).then_inc(am["latsq"], 1)
                split_next(g + 1, (g + 1) % RAW)
                latent(Q_LORA_T, False, 1.0 / (Q_LORA_T * P))
                for p in range(6):
                    if p % 2 == 0:
                        act.wait_ge(am["qraw"], p // 2 + 1)
                    else:
                        act.wait_ge(w_used, g + 2 + p // 2 + 1)
                    dst = qn[:, 2 * p:2 * p + 2, :] if p < 4 else qr[:, 2 * p - 8:2 * p - 6, :]
                    A(dst, bank[p % 2][:, :].rearrange("p (e t) -> p e t", e=2), ACT.Copy).then_inc(am["qev"], 1)
                    if p % 2:
                        split_next(g + 2 + p // 2, (g + 2 + p // 2) % RAW)
                act.wait_ge(am["qev"], 6)
                for c in range(2):
                    A(sqr[:, 2 * c:2 * c + 2, :], qr[:, 2 * c:2 * c + 2, :], ACT.Square).then_inc(am["ropesq"], 1)
                head_norms(qn, False)
                A(warm[:, 3:4], epsc[:, 3:4], ACT.Exp)
                for i in range(HEADS + 2):
                    if i < HEADS:
                        act.wait_ge(am["max"], i + 1)
                        e = i % 2
                        A(prb[:, e, 0:P], bank[e][:, 0:P], ACT.Exp, bias=st[:, e, 0:1], accum_out=st[:, e, 2:3])
                        A(prb[:, e, P:P + T], bank[e][:, T:2 * T], ACT.Exp, bias=st[:, e, 1:2],
                          accum_out=st[:, e, 3:4]).then_inc(am["exp"], 1)
                    if 1 <= i <= HEADS:
                        act.wait_ge(am["turned"], i)
                        A(pt[:, (i - 1) % 2, :], bank[4 + (i - 1) % 2][:, 0:384], ACT.Copy).then_inc(am["pt"], 1)
                    if i >= 2:
                        act.wait_ge(am["o"], i - 1)
                        A(hh[:, i - 2, :], half(6 + i % 2, 0), ACT.Copy).then_inc(am["ohi"], 1)
                for g in range(G_MLA_OUT, G_MLA_OUT + PROJ_OUT):
                    split_next(g, g % RAW)

            act.wait_ge(consts_in, 64)
            act.wait_ge(set_consts, 1)
            A(cact[:, :], craw[:, :], ACT.Silu).then_inc(c_ready, 1)
            act.wait_ge(am["angle"], 1)
            A(cs[:, :, :], ang[:, 4:6, :], ACT.Sin).then_inc(am["sin"], 1)
            split_hi(0, 0, True)
            split_hi(1, 1, True)
            stats(0)
            A(warm[:, 1:2], epsc[:, 3:4], ACT.Silu)
            modulate(0, mod_index(0, 0))
            ffn(0)
            stats(1)
            A(warm[:, 1:2], epsc[:, 3:4], ACT.Silu)
            modulate(1, mod_index(0, 3))
            gdn()
            stats(2)
            A(warm[:, 1:2], epsc[:, 3:4], ACT.Silu)
            modulate(2, mod_index(0, 6))
            ffn(1)
            stats(3)
            modulate(3, 9)
            kv()
            modulate(4, mod_index(1, 0))
            ffn(2)
            stats(4)
            modulate(5, mod_index(1, 3))
            mla()
            stats(5)
            A(warm[:, 1:2], epsc[:, 3:4], ACT.Silu)
            modulate(6, mod_index(1, 6))
            ffn(3)

        @block.vector
        def _(dve):
            V = nc.vector
            links = [0]

            def link(ins):
                links[0] += 1
                ins.then_inc(dve_link, 1)
                dve.wait_ge(dve_link, links[0])

            def split_lo(g, r):
                dve.wait_ge(w_hi, g + 1)
                V.tensor_tensor(wl[:, r % 2, :], raw[:, r, :], wh[:, r % 2, :].bitcast(F32), ALU.subtract).then_inc(w_lo, 1)

            def split_next(g, r):
                if isinstance(g, int) and g + 2 >= granules:
                    return
                split_lo(g + 2, (r + 2) % RAW)

            def ada_finish(u):
                dve.wait_ge(ada_red, u)
                V.tensor_tensor(mods[:, bass.ds(u * 2 - 2, 2)], bank[3][:, 0:2], modb[:, bass.ds(u * 2 - 2, 2)],
                                ALU.add).then_inc(ada_done, 1)

            def ada_step(u, par, first=False):
                if not first:
                    ada_finish(u)
                dve.wait_ge(ada_landed[par], u * 8 + (16 - 8 * par))
                V.tensor_scalar(acc[:, :], araw[:, par, 0, :], cact[:, 0:1], None, ALU.mult).then_inc(ada_mac, 1)
                for k in range(1, KD):
                    dve.wait_ge(ada_mac, u * KD + k)
                    V.scalar_tensor_tensor(out=acc[:, :], in0=araw[:, par, k, :], scalar=cact[:, k:k + 1], in1=acc[:, :],
                                           op0=ALU.mult, op1=ALU.add).then_inc(ada_mac, 1)

            def residual(stage, vec, factor, g_last):
                s = out_stages[stage]
                dve.wait_ge(ada_done, 4 * (vec + 1))
                link(V.tensor_scalar(gate[:, :], mods[:, 8 * vec:8 * vec + 8], factor, None, ALU.mult))
                for m in range(KD):
                    if m % 2 == 0 and m < KD - 2:
                        dve.wait_ge(y_done, 3 * s + m // 2 + 1)
                    elif m == KD - 2:
                        dve.wait_ge(w_used, g_last + 1)
                    V.scalar_tensor_tensor(out=x[:, m, :], in0=half(4 + m // 2, m % 2), scalar=gate[:, m:m + 1],
                                           in1=x[:, m, :], op0=ALU.mult, op1=ALU.add).then_inc(x_upd, 1)

            def gains(vec, c0):
                dve.wait_ge(ada_done, 4 * (vec + 2))
                link(V.scalar_tensor_tensor(out=gs[:, :], in0=mods[:, 8 * vec + 8:8 * vec + 16], scalar=1.0,
                                            in1=col[:, c0:c0 + 8], op0=ALU.add, op1=ALU.mult))

            def norm(v):
                dve.wait_ge(std_ready, v + 1)
                link(V.reciprocal(rstd[:, :], std[:, 0, 0:T]))

            def modulate(n):
                if n == 4:
                    dve.wait_ge(w_used, G_KV + 2)
                for m in range(KD + 1):
                    if m < KD:
                        if 8 * n + m >= 2:
                            dve.wait_ge(hh_ready, 8 * n + m - 1)
                        V.tensor_tensor(t2[:, m % 2, :], x[:, m, :], rstd[:, :], ALU.mult).then_inc(mod_t, 1)
                    if m:
                        dve.wait_ge(hh_ready, 8 * n + m)
                        V.tensor_tensor(hl[:, m - 1, :], h32[:, (m - 1) % 2, :], hh[:, m - 1, :].bitcast(F32),
                                        ALU.subtract).then_inc(h_ready, 1)

            def ffn_in_step(f, g, j, r, par, unit=None):
                dve.wait_ge(ff_silu, j + (22 * f + 1))
                V.tensor_tensor(hid[:, par, :], silu[:, par, :], half(par, 1), ALU.mult).then_inc(ff_hid, 1)
                split_next(g, r)
                dve.wait_ge(ff_hi, j + (22 * f + 1))
                V.tensor_tensor(fl[:, j, :], hid[:, par, :], fh[:, j, :].bitcast(F32), ALU.subtract).then_inc(ff_lo, 1)
                if unit is not None:
                    ada_step(*unit)

            def ffn(f, u0):
                g0 = G_FFN[f]
                for j in (0, 1):
                    unit = (u0, u0 % 2) if u0 is not None and j else None
                    ffn_in_step(f, g0 + j, j, (g0 + j) % RAW, j, unit)
                with dve.Fori(0, 5) as i:
                    for q in range(4):
                        unit = None
                        if u0 is not None and q % 2:
                            u = u0 + 1 + q // 2
                            unit = (i * 2 + u, u % 2)
                        ffn_in_step(f, i * 4 + (g0 + 2 + q), i * 4 + (2 + q), (g0 + 2 + q) % RAW, q % 2, unit)
                g1 = g0 + FFN_IN
                turns = 1 if g1 + FFN_OUT == granules else 2
                split_next(g1, g1 % RAW)
                with dve.Fori(0, turns) as i:
                    for q in range(4):
                        split_next(i * 4 + (g1 + 1 + q), (g1 + 1 + q) % RAW)
                        if u0 is not None:
                            ada_step(i * 4 + (u0 + 11 + q), (u0 + 11 + q) % 2)
                for o in range(1 + 4 * turns, FFN_OUT):
                    split_next(g1 + o, (g1 + o) % RAW)
                    if u0 is not None and o <= 8:
                        ada_step(u0 + 10 + o, (u0 + 10 + o) % 2)

            def conv(t0, e, par):
                dve.wait_ge(gc_first, t0 + 2)
                for d in range(1, 4):
                    if d > 1:
                        dve.wait_ge(gc_tap, t0 * 2 + (2 * e + d - 1))
                    V.scalar_tensor_tensor(out=silu[:, e, d:T], in0=bank[par][:, e * T:(e + 1) * T - d],
                                           scalar=col[:, bass.ds(t0 + (C_CONV + 24 * (3 - d) + e), 1)], in1=silu[:, e, d:T],
                                           op0=ALU.mult, op1=ALU.add).then_inc(gc_tap if d < 3 else gc_conv, 1)

            def gdn(u0):
                dve.wait_ge(ba_hi, 1)
                V.tensor_tensor(wbal[:, :, :], wba[:, :, :], wbah[:, :, :].bitcast(F32), ALU.subtract).then_inc(ba_lo, 1)

                def tile_pair(g, r, t0, par, unit):
                    conv(t0, 0, par)
                    conv(t0, 1, par)
                    split_next(g, r)
                    if unit is not None:
                        ada_step(*unit)

                for n in range(4):
                    g = G_GDN + n
                    tile_pair(g, g % RAW, 2 * n, n % 2, (u0 + n // 2, (u0 + n // 2) % 2) if n % 2 else None)
                with dve.Fori(0, 2) as i:
                    for n in range(4, 8):
                        u = u0 + n // 2
                        tile_pair(i * 4 + (G_GDN + n), (G_GDN + n) % RAW, i * 8 + 2 * n, n % 2,
                                  (i * 2 + u, u % 2) if n % 2 else None)
                dve.wait_ge(ba_done, 1)
                z16 = bank[2][:, 0:32].rearrange("p (b c) -> p b c", b=2)
                V.tensor_tensor(sc[:, 6, :, :], z16[:, :, 8:16], wide(tokc[:, 0:8], 2), ALU.add)
                V.tensor_copy(sc[:, 7, :, :], z16[:, :, 0:8]).then_inc(gt_dve, 1)
                dve.wait_ge(gt_act, 1)
                link(V.tensor_scalar(sc[:, 13, :, :], sc[:, 8, :, :], 1.0, None, ALU.add))
                V.reciprocal(sc[:, 0, :, :], sc[:, 13, :, :])
                link(V.scalar_tensor_tensor(out=sc[:, 5, :, :], in0=sc[:, 6, :, :], scalar=0.0, in1=sc[:, 11, :, :],
                                            op0=ALU.max, op1=ALU.add))
                V.scalar_tensor_tensor(out=sc[:, 1, :, :], in0=sc[:, 5, :, :], scalar=-1.0, in1=wide(sc[:, 12, 0, :], 2),
                                       op0=ALU.mult, op1=ALU.mult).then_inc(gt_dve, 1)
                for n in range(12, 16):
                    g = G_GDN + n
                    split_next(g, g % RAW)
                    if n % 2:
                        u = u0 + n // 2
                        ada_step(u, u % 2)
                dve.wait_ge(gt_act, 2)
                V.tensor_copy(sc[:, 2, :, :], bank[2][:, 32:48].rearrange("p (b h) -> p b h", b=2))
                link(V.tensor_tensor(sc[:, 5, :, :], sc[:, 0, :, :], sc[:, 3, :, :], ALU.mult))
                for p in range(8):
                    dve.wait_ge(l2_std, p + 1)
                    link(V.reciprocal(std[:, p % 2, :], std[:, p % 2, :]))
                    V.tensor_tensor(qkv[:, 2 * p:2 * p + 2, :], qkv[:, 2 * p:2 * p + 2, :],
                                    std[:, p % 2, :].rearrange("p (e t) -> p e t", e=2), ALU.mult).then_inc(l2_done, 1)
                for hg in range(2):
                    hs = slice(4 * hg, 4 * hg + 4)
                    for b in range(2):
                        s = 2 * hg + b
                        if b:
                            dve.wait_ge(co["kq"], s)
                        gcol = sc[:, 1, b, hs].unsqueeze(2).to_broadcast([P, 4, P])
                        bcol = sc[:, 0, b, hs].unsqueeze(2).to_broadcast([P, 4, P])
                        V.tensor_tensor(heads4(TMP[:, 0, :]), wide(mat[:, M_LE, :], 4), gcol, ALU.mult)
                        V.tensor_tensor(heads4(TMP[:, 1, :]), wide(mat[:, M_ID, :], 4), bcol, ALU.mult).then_inc(co["gm"], 1)
                        dve.wait_ge(co["kq"], s + 1)
                        V.tensor_tensor(heads4(BS[:, b, :]), heads4(bank[2][:, :]), wide(mat[:, M_ST, :], 4), ALU.mult).then_inc(co["bs"], 1)
                        for h in range(4):
                            ins = V.tensor_scalar(DC[:, b, P * h:P * h + P], bank[6 + b][:, P * h:P * h + P],
                                                  sc[:, 2, b, 4 * hg + h:4 * hg + h + 1], 0.0, ALU.subtract, ALU.min)
                        ins.then_inc(co["dd"], 1)
                        dve.wait_ge(co["decay"], s + 1)
                        link(V.tensor_tensor(heads4(DC[:, b, :]), heads4(DC[:, b, :]), wide(mat[:, M_LE, :], 4), ALU.mult))
                        link(V.tensor_tensor(LT[:, b, :], bank[b][:, :], DC[:, b, :], ALU.mult))
                        V.tensor_tensor(AT[:, b, :], bank[4 + b][:, :], DC[:, b, :], ALU.mult)
                        if b:
                            V.tensor_tensor(heads4(QG[:, :]), heads4(QG[:, :]), qkv[:, hs, b * P:(b + 1) * P], ALU.mult)
                        V.tensor_tensor(LT[:, b, :], LT[:, b, :], BS[:, b, :], ALU.mult).then_inc(co["lt"], 1)
                    for b in range(2):
                        s = 2 * hg + b
                        dve.wait_ge(co["turned"], s + 1)
                        V.tensor_tensor(heads4(X[:, b, :]), heads4(bank[b][:, :]), wide(mat[:, M_LV, :], 4), ALU.mult)
                        link(V.tensor_tensor(heads4(XT[:, b, :]), heads4(LT[:, b, :]), wide(mat[:, M_LVT, :], 4), ALU.mult))
                        V.tensor_tensor(heads4(X[:, b, :]), wide(mat[:, M_ID, :], 4), heads4(X[:, b, :]), ALU.subtract)
                        V.tensor_tensor(heads4(XT[:, b, :]), wide(mat[:, M_ID, :], 4), heads4(XT[:, b, :]), ALU.subtract).then_inc(inv_x[b], 1)
                        for h in range(4):
                            hc = slice(P * h, P * h + P)
                            hx = 4 * hg + h
                            V.tensor_scalar(RV[:, b, hc], bank[6 + b][:, hc], sc[:, 0, b, hx:hx + 1], None, ALU.mult)
                            dst, c = (KDC, 4) if b == 0 else (RK, 5)
                            ins = V.tensor_scalar(dst[:, hc], bank[4 + b][:, hc], sc[:, c, b, hx:hx + 1], None, ALU.mult)
                        ins.then_inc(co["tokd"], 1)

                    def level(lv, n):
                        for b in range(2):
                            dve.wait_ge(inv_p[b], n)
                            V.tensor_tensor(heads4(PS[:, b, :]), heads4(bank[b][:, :]),
                                            mat[:, bass.ds(lv + M_LV, 1), :].to_broadcast([P, 4, P]), ALU.mult).then_inc(inv_ps[b], 1)
                        for b in range(2):
                            dve.wait_ge(inv_xp[b], n)
                            V.tensor_tensor(X[:, b, :], X[:, b, :], bank[4 + b][:, :], ALU.subtract)
                            V.tensor_tensor(XT[:, b, :], XT[:, b, :], bank[6 + b][:, :], ALU.subtract).then_inc(inv_x[b], 1)

                    with dve.Fori(1, LEVELS - 1) as lv:
                        level(lv, lv + hg * 6)
                    n = 6 + 6 * hg
                    for b in range(2):
                        dve.wait_ge(inv_p[b], n)
                        V.tensor_tensor(heads4(PS[:, b, :]), heads4(bank[b][:, :]), wide(mat[:, M_LV + LEVELS - 1, :], 4),
                                        ALU.mult).then_inc(inv_ps[b], 1)
                    for b in range(2):
                        dve.wait_ge(inv_xp[b], n)
                        V.tensor_tensor(XT[:, b, :], XT[:, b, :], bank[6 + b][:, :], ALU.subtract).then_inc(inv_x[b], 1)
                    for b in range(2):
                        s = 2 * hg + b
                        dve.wait_ge(co["u"], s + 1)
                        if b:
                            V.tensor_copy(WT[:, :], bank[4 + b][:, :])
                        V.tensor_copy(U[:, b, :], bank[b][:, :]).then_inc(co["uu"], 1)
                    dve.wait_ge(co["state"], hg + 1)
                    V.tensor_copy(SS[:, :], bank[6][:, :]).then_inc(co["state_sb"], 1)
                    dve.wait_ge(co["ws"], hg + 1)
                    V.tensor_tensor(U[:, 1, :], U[:, 1, :], bank[7][:, :], ALU.subtract).then_inc(co["vnew"], 1)
                    for p in range(2):
                        q = 2 * hg + p
                        o3 = O32[:, 2 * p:2 * p + 2, :]
                        dve.wait_ge(co["ostd"], q + 1)
                        link(V.reciprocal(std[:, p, :], std[:, p, :]))
                        link(V.scalar_tensor_tensor(out=o3, in0=o3, scalar=col[:, C_GDNN:C_GDNN + 1],
                                                    in1=std[:, p, :].rearrange("p (e t) -> p e t", e=2), op0=ALU.mult, op1=ALU.mult))
                        V.tensor_tensor(o3, o3, zs[:, 2 * q:2 * q + 2, :], ALU.mult).then_inc(co["onorm"], 1)
                    for p in range(2):
                        q = 2 * hg + p
                        dve.wait_ge(co["ohi"], q + 1)
                        V.tensor_tensor(hl[:, 2 * q:2 * q + 2, :], O32[:, 2 * p:2 * p + 2, :],
                                        hh[:, 2 * q:2 * q + 2, :].bitcast(F32), ALU.subtract).then_inc(co["olo"], 1)
                for g in range(G_GDN_OUT, G_GDN_OUT + PROJ_OUT):
                    split_next(g, g % RAW)

            def angles():
                dve.wait_ge(pos_in, 16)
                dve.wait_ge(consts_in, 64)
                C1 = 6.28125
                C2 = 0.0019350051879882812
                C3 = TWO_PI - C1 - C2
                link(V.tensor_copy(ang[:, 0, :], angi[:, :]))
                link(V.tensor_scalar(ang[:, 1, :], ang[:, 0, :], col[:, C_FREQ:C_FREQ + 1], None, ALU.mult))
                link(V.tensor_scalar(ang[:, 2, :], ang[:, 1, :], 1.0 / TWO_PI, RND, ALU.mult, ALU.add))
                link(V.tensor_scalar(ang[:, 3, :], ang[:, 2, :], RND, None, ALU.subtract))
                for c in (C1, C2, C3):
                    link(V.scalar_tensor_tensor(out=ang[:, 1, :], in0=ang[:, 3, :], scalar=-c, in1=ang[:, 1, :],
                                                op0=ALU.mult, op1=ALU.add))
                link(V.tensor_scalar(ang[:, 2, :], ang[:, 1, :], TWO_PI / 4, None, ALU.add))
                link(V.tensor_scalar(ang[:, 3, :], ang[:, 2, :], TWO_PI / 2, None, ALU.is_gt))
                link(V.scalar_tensor_tensor(out=ang[:, 2, :], in0=ang[:, 3, :], scalar=-TWO_PI, in1=ang[:, 2, :],
                                            op0=ALU.mult, op1=ALU.add))
                V.tensor_scalar(ang[:, 4, :], ang[:, 2, :], 3.1415925, -3.1415925, ALU.min, ALU.max)
                V.tensor_scalar(ang[:, 5, :], ang[:, 1, :], 3.1415925, -3.1415925, ALU.min, ALU.max).then_inc(am["angle"], 1)
                dve.wait_ge(am["sin"], 1)
                V.tensor_scalar(cs[:, 1, :], cs[:, 1, :], col[:, C_SIGN:C_SIGN + 1], None, ALU.mult).then_inc(dve_link, 1)
                links[0] += 1

            def latent(nt, first):
                dve.wait_ge(am["latstd"], 1 if first else 2)
                link(V.reciprocal(rot[:, 0:T], std[:, 0, 0:T]))
                i0 = 0 if first else 2
                for i in range(nt):
                    V.tensor_tensor(lat[:, i, :], lat[:, i, :], rot[:, 0:T], ALU.mult).then_inc(am["latn"], 1)
                for i in range(nt):
                    dve.wait_ge(am["lathi"], i0 + i + 1)
                    V.tensor_tensor(latl[:, i, :], h32[:, i % 2, :], lath[:, i, :].bitcast(F32), ALU.subtract).then_inc(am["latlo"], 1)

            def rotary(src, n, c0, gain):
                w = src.shape[1] // n
                for c in range(n):
                    part = src[:, c * w:(c + 1) * w, :]
                    V.tensor_scalar(part, part, gain, None, ALU.mult).then_inc(am["gained"], 1)
                dve.wait_ge(am["gained"], c0 + n)
                for c in range(n):
                    part = src[:, c * w:(c + 1) * w, :]
                    tmp = rot[:, 0:w * T].rearrange("p (e t) -> p e t", e=w)
                    dve.wait_ge(am["swap"], c0 + c + 1)
                    V.tensor_tensor(tmp, swap_bank(n, c)[:, 0:w * T].rearrange("p (e t) -> p e t", e=w), wide(cs[:, 1, :], w), ALU.mult)
                    link(V.tensor_tensor(part, part, wide(cs[:, 0, :], w), ALU.mult))
                    link(V.tensor_tensor(part, part, tmp, ALU.add))

            def head_norms(nope, rope_in, rope_out, c, first):
                p0 = 0 if first else 4
                for j in range(4):
                    dve.wait_ge(am["hstd"], p0 + j + 1)
                    r = std[:, j % 2, :]
                    link(V.reciprocal(r, r))
                    for e in range(2):
                        hp = slice(64 * e, 64 * e + 64)
                        V.tensor_tensor(rope_out[hp, j, :], rope_in[hp, 0 if first else j, :], r[hp, e * T:(e + 1) * T], ALU.mult)
                    V.scalar_tensor_tensor(out=nope[:, 2 * j:2 * j + 2, :], in0=nope[:, 2 * j:2 * j + 2, :], scalar=col[:, c:c + 1],
                                           in1=r.rearrange("p (e t) -> p e t", e=2), op0=ALU.mult, op1=ALU.mult).then_inc(am["hn"], 1)

            def kv():
                g = G_KV
                split_next(g, g % RAW)
                split_next(g + 1, (g + 1) % RAW)
                latent(KV_LORA_T, True)
                dve.wait_ge(am["ropesq"], 1)
                rotary(lat[:, 2:3, :], 1, 0, col[:, C_KN + 1:C_KN + 2])
                split_next(g + 2, (g + 2) % RAW)
                split_next(g + 3, (g + 3) % RAW)
                head_norms(kn, lat[:, 2:3, :], kr, C_KN, True)

            def mla(u0):
                g = G_MLA
                split_next(g, g % RAW)
                ada_step(u0, u0 % 2)
                split_next(g + 1, (g + 1) % RAW)
                latent(Q_LORA_T, False)
                for p in range(3):
                    split_next(g + 2 + p, (g + 2 + p) % RAW)
                    ada_step(u0 + 1 + p, (u0 + 1 + p) % 2)
                dve.wait_ge(am["ropesq"], 3)
                rotary(qr[:, :, :], 2, 1, col[:, C_QN + 1:C_QN + 2])
                head_norms(qn, qr, qr, C_QN, False)
                for i in range(HEADS + 3):
                    if i < HEADS:
                        e = i % 2
                        dve.wait_ge(am["s"], i + 1)
                        V.memset(bank[e][0:64, 64:128], NEG)
                        link(V.memset(bank[e][0:64, 448:512], NEG))
                        V.tensor_reduce(st[:, e, 0:1], bank[e][:, 0:P], AX, ALU.max, negate=True)
                        V.tensor_reduce(st[:, e, 1:2], bank[e][:, T:2 * T], AX, ALU.max, negate=True).then_inc(am["max"], 1)
                        dve.wait_ge(am["exp"], i + 1)
                        link(V.reciprocal(st[:, e, 4:6], st[:, e, 2:4]))
                        V.tensor_scalar(prb[:, e, 0:P], prb[:, e, 0:P], st[:, e, 4:5], None, ALU.mult)
                        V.tensor_scalar(prb[:, e, P:P + T], prb[:, e, P:P + T], st[:, e, 5:6], None, ALU.mult).then_inc(am["p"], 1)
                    if i >= 3:
                        dve.wait_ge(am["ohi"], i - 2)
                        V.tensor_tensor(hl[:, i - 3, :], half(6 + (i - 3) % 2, 0), hh[:, i - 3, :].bitcast(F32),
                                        ALU.subtract).then_inc(am["olo"], 1)
                for n in range(PROJ_OUT):
                    split_next(G_MLA_OUT + n, (G_MLA_OUT + n) % RAW)
                    if n < 2:
                        ada_step(u0 + 4 + n, (u0 + 4 + n) % 2)
                ada_finish(u0 + 6)

            angles()
            dve.wait_ge(c_ready, 1)
            ada_step(0, 0, first=True)
            for u in range(1, ADA_FIRST):
                if u == 3:
                    split_lo(0, 0)
                    split_lo(1, 1)
                ada_step(u, u % 2)
            gains(0, C_NORM)
            norm(0)
            modulate(0)
            ffn(0, ADA_FIRST)
            residual("ffn0", mod_index(0, 2), 0.5, G_FFN[0] + 32)
            gains(mod_index(0, 3), C_NORM + 8)
            norm(1)
            modulate(1)
            gdn(ADA_FIRST + 19)
            residual("gdn", mod_index(0, 5), 1.0, G_GDN_OUT + 3)
            gains(mod_index(0, 6), C_NORM + 16)
            norm(2)
            modulate(2)
            ffn(1, ADA_FIRST + 27)
            residual("ffn1", mod_index(0, 8), 0.5, G_FFN[1] + 32)
            gains(9, C_KVN)
            norm(3)
            modulate(3)
            kv()
            gains(mod_index(1, 0), C_NORM + 24)
            modulate(4)
            ffn(2, ADA_FIRST + 46)
            residual("ffn2", mod_index(1, 2), 0.5, G_FFN[2] + 32)
            gains(mod_index(1, 3), C_NORM + 32)
            norm(4)
            modulate(5)
            mla(ADA_FIRST + 65)
            residual("mla", mod_index(1, 5), 1.0, G_MLA_OUT + 3)
            gains(mod_index(1, 6), C_NORM + 40)
            norm(5)
            modulate(6)
            ffn(3, None)
            residual("ffn3", mod_index(1, 8), 0.5, G_FFN[3] + 32)

        @block.tensor
        def _(pe):
            M = nc.tensor.matmul

            def col_tile(dst, slot, i0, nk, src_h, src_l, ready=None, start=True):
                for k in range(nk):
                    if ready is not None:
                        pe.wait_ge(ready[0], ready[1] + k + 1)
                    w = slice((i0 + k) * P, (i0 + k + 1) * P)
                    M(dst, wh[:, slot, w], src_h[:, k, :], start=start and k == 0, stop=False)
                    M(dst, wh[:, slot, w], src_l[:, k, :], start=False, stop=False)
                    ins = M(dst, wl[:, slot, w], src_h[:, k, :], start=False, stop=k == nk - 1)
                return ins

            def ada_reduce(u):
                pe.wait_ge(ada_mac, u * KD + KD)
                if not (isinstance(u, int) and u == 0):
                    pe.wait_ge(ada_done, u)
                M(bank[3][:, 0:1], acc[:, 0:P], ones[:, 0:1], start=True, stop=True)
                M(bank[3][:, 1:2], acc[:, P:2 * P], ones[:, 0:1], start=True, stop=True).then_inc(ada_red, 1)

            def stats(v):
                for m in range(KD):
                    pe.wait_ge(sq_ready, 8 * v + m + 1)
                    M(half(2, 0), mean_d[:, :], sq[:, m % 2, 0:T], start=m == 0, stop=m == KD - 1).then_inc(ss_mm, 1)

            def ffn_in_step(f, g, j, slot, par, n=None, unit=None):
                pe.wait_ge(w_lo, g + 1)
                if not (isinstance(j, int) and 22 * f + j < 2):
                    pe.wait_ge(ff_hid, j + (22 * f - 1))
                col_tile(half(par, 0), slot, 0, KD, hh, hl, None if n is None else (h_ready, 8 * n))
                col_tile(half(par, 1), slot, KD, KD, hh, hl).then_inc(w_used, 1)
                if unit is not None:
                    ada_reduce(unit)

            def out_step(g, slot, kt, src_h, src_l, first=False, last=False, unit=None):
                for m in range(KD):
                    dst = half(4 + m // 2, m % 2)
                    for k in range(2):
                        w = slice((k * KD + m) * P, (k * KD + m + 1) * P)
                        M(dst, wh[:, slot, w], src_h[:, kt + k, :], start=first and k == 0 and m % 2 == 0, stop=False,
                          skip_group_check=True)
                        M(dst, wh[:, slot, w], src_l[:, kt + k, :], start=False, stop=False, skip_group_check=True)
                        ins = M(dst, wl[:, slot, w], src_h[:, kt + k, :], start=False, stop=last and k == 1,
                                skip_group_check=True)
                    if last and m % 2 and m < KD - 1:
                        ins.then_inc(y_done, 1)
                ins.then_inc(w_used, 1)
                if unit is not None:
                    ada_reduce(unit)

            def ffn(f, n, u0):
                g0 = G_FFN[f]
                for j in (0, 1):
                    unit = u0 - 1 if u0 is not None and j else None
                    ffn_in_step(f, g0 + j, j, (g0 + j) % 2, j, n if j == 0 else None, unit)
                with pe.Fori(0, 5) as i:
                    for q in range(4):
                        unit = i * 2 + (u0 + q // 2) if u0 is not None and q % 2 else None
                        ffn_in_step(f, i * 4 + (g0 + 2 + q), i * 4 + (2 + q), (g0 + 2 + q) % 2, q % 2, unit=unit)
                g1 = g0 + FFN_IN
                turns = 1 if g1 + FFN_OUT == granules else 2

                def step(o, g, slot, unit, **kw):
                    pe.wait_ge(w_lo, g + 1)
                    pe.wait_ge(ff_lo, o * 2 + (22 * f + 2))
                    out_step(g, slot, o * 2, fh, fl, unit=unit, **kw)

                step(0, g1, g1 % 2, None, first=True)
                with pe.Fori(0, turns) as i:
                    for q in range(4):
                        step(i * 4 + (1 + q), i * 4 + (g1 + 1 + q), (g1 + 1 + q) % 2,
                             i * 4 + (u0 + 10 + q) if u0 is not None else None)
                for o in range(1 + 4 * turns, FFN_OUT):
                    step(o, g1 + o, (g1 + o) % 2, u0 + 9 + o if u0 is not None and o <= 8 else None, last=o == FFN_OUT - 1)

            def project(g0, ready, count, units_at=()):
                pe.wait_ge(ready, count)
                for n in range(PROJ_OUT):
                    g = g0 + n
                    pe.wait_ge(w_lo, g + 1)
                    out_step(g, g % 2, 2 * n, hh, hl, first=n == 0, last=n == PROJ_OUT - 1,
                             unit=units_at[n] if n < len(units_at) else None)

            def gdn(n, u0):
                pe.wait_ge(ba_lo, 1)
                pe.wait_ge(h_ready, 8 * n + 8)
                for b in range(2):
                    dst = bank[2][:, 16 * b:16 * b + 16]
                    for k in range(KD):
                        ht = slice(b * P, b * P + P)
                        M(dst, hh[:, k, ht], wbah[:, k, :], start=k == 0, stop=False)
                        M(dst, hl[:, k, ht], wbah[:, k, :], start=False, stop=False)
                        ins = M(dst, hh[:, k, ht], wbal[:, k, :], start=False, stop=k == KD - 1)
                ins.then_inc(ba_done, 1)

                def tile_pair(g, slot, par, free, unit):
                    pe.wait_ge(w_lo, g + 1)
                    if free is not None:
                        pe.wait_ge(*free)
                    col_tile(half(par, 0), slot, 0, KD, hh, hl)
                    col_tile(half(par, 1), slot, KD, KD, hh, hl).then_inc(w_used, 1)
                    if unit is not None:
                        ada_reduce(unit)

                for m in range(4):
                    g = G_GDN + m
                    tile_pair(g, g % 2, m % 2, (gc_conv, 2 * m - 2) if m > 1 else None, u0 - 1 + m // 2 if m % 2 else None)
                with pe.Fori(0, 2) as i:
                    for m in range(4, 8):
                        g = G_GDN + m
                        tile_pair(i * 4 + g, g % 2, m % 2, (gc_conv, i * 8 + (2 * m - 2)), i * 2 + (u0 - 1 + m // 2) if m % 2 else None)
                for m in range(12, 16):
                    g = G_GDN + m
                    tile_pair(g, g % 2, m % 2, (gc_conv, 2 * m - 2) if m < 14 else (gz_silu, m - 13), u0 - 1 + m // 2 if m % 2 else None)
                pe.wait_ge(gt_dve, 2)
                for b in range(2):
                    M(bank[2][:, 32 + 8 * b:40 + 8 * b], mat[:, M_LE, :], sc[:, 1, b, :], start=True, stop=True)
                    ins = M(bank[2][:, 48 + 8 * b:56 + 8 * b], mat[:, M_GT, :], sc[:, 1, b, :], start=True, stop=True)
                ins.then_inc(gt_pe, 1)
                pe.wait_ge(gz_silu, 4)
                for p in range(8):
                    pe.wait_ge(l2_sq, p + 1)
                    if p >= 2:
                        pe.wait_ge(l2_std, p - 1)
                    M(bank[p % 2][:, :], ones[:, :], sq[:, p % 2, :], start=True, stop=True).then_inc(l2_ss, 1)
                pe.wait_ge(l2_done, 8)
                for hg in range(2):
                    def kq(which, h, b):
                        return qkv[:, 8 * which + 4 * hg + h, b * P:b * P + P]

                    def cols4(h):
                        return slice(P * h, P * h + P)

                    for b in range(2):
                        s = 2 * hg + b
                        pe.wait_ge(co["gm"], s + 1)
                        if s:
                            pe.wait_ge(co["bs"], s)
                        if hg:
                            pe.wait_ge(co["olo"], 2)
                        for h in range(4):
                            M(bank[b][:, cols4(h)], kq(1, h, b), kq(1, h, b), start=True, stop=True)
                        for h in range(4):
                            M(bank[4 + b][:, cols4(h)], kq(1, h, b), kq(0, h, b), start=True, stop=True)
                        M(bank[2][:, :], ones[:, :], TMP[:, 1, :], start=True, stop=True)
                        M(bank[6 + b][:, :], ones[:, :], TMP[:, 0, :], start=True, stop=True).then_inc(co["kq"], 1)
                    for b in range(2):
                        s = 2 * hg + b
                        pe.wait_ge(co["lt"], s + 1)
                        for h in range(4):
                            nc.tensor.transpose(bank[4 + b][:, cols4(h)], kq(1, h, b), mat[:, M_ID, :])
                        for h in range(4):
                            nc.tensor.transpose(bank[6 + b][:, cols4(h)], kq(2, h, b), mat[:, M_ID, :])
                        for h in range(4):
                            ins = nc.tensor.transpose(bank[b][:, cols4(h)], LT[:, b, cols4(h)], mat[:, M_ID, :])
                        ins.then_inc(co["turned"], 1)

                    pe.wait_ge(co["tokd"], 2 * hg + 2)
                    with pe.Fori(1, LEVELS - 1) as lv:
                        for b in range(2):
                            pe.wait_ge(inv_x[b], lv + 7 * hg)
                            for h in range(4):
                                ins = M(bank[b][:, cols4(h)], LT[:, b, cols4(h)], X[:, b, cols4(h)], start=True, stop=True)
                            ins.then_inc(inv_p[b], 1)
                        for b in range(2):
                            pe.wait_ge(inv_ps[b], lv + 6 * hg)
                            for h in range(4):
                                M(bank[4 + b][:, cols4(h)], XT[:, b, cols4(h)], PS[:, b, cols4(h)], start=True, stop=True)
                            for h in range(4):
                                ins = M(bank[6 + b][:, cols4(h)], PS[:, b, cols4(h)], XT[:, b, cols4(h)], start=True, stop=True)
                            ins.then_inc(inv_xp[b], 1)
                    for b in range(2):
                        pe.wait_ge(inv_x[b], 6 + 7 * hg)
                        for h in range(4):
                            ins = M(bank[b][:, cols4(h)], LT[:, b, cols4(h)], X[:, b, cols4(h)], start=True, stop=True)
                        ins.then_inc(inv_p[b], 1)
                    for b in range(2):
                        pe.wait_ge(inv_ps[b], 6 + 6 * hg)
                        for h in range(4):
                            ins = M(bank[6 + b][:, cols4(h)], PS[:, b, cols4(h)], XT[:, b, cols4(h)], start=True, stop=True)
                        ins.then_inc(inv_xp[b], 1)
                    for b in range(2):
                        s = 2 * hg + b
                        pe.wait_ge(inv_x[b], 7 + 7 * hg)
                        if b:
                            for h in range(4):
                                M(bank[4 + b][:, cols4(h)], RK[:, cols4(h)], XT[:, b, cols4(h)], start=True, stop=True)
                        for h in range(4):
                            ins = M(bank[b][:, cols4(h)], XT[:, b, cols4(h)], RV[:, b, cols4(h)], start=True, stop=True)
                        ins.then_inc(co["u"], 1)
                    pe.wait_ge(co["uu"], 2 * hg + 1)
                    for h in range(4):
                        ins = M(bank[6][:, cols4(h)], KDC[:, cols4(h)], U[:, 0, cols4(h)], start=True, stop=True)
                    ins.then_inc(co["state"], 1)
                    for h in range(4):
                        ins = M(bank[4][:, cols4(h)], U[:, 0, cols4(h)], AT[:, 0, cols4(h)], start=True, stop=True)
                    ins.then_inc(co["o0"], 1)
                    pe.wait_ge(co["state_sb"], hg + 1)
                    pe.wait_ge(co["uu"], 2 * hg + 2)
                    for h in range(4):
                        ins = M(bank[7][:, cols4(h)], WT[:, cols4(h)], SS[:, cols4(h)], start=True, stop=True)
                    ins.then_inc(co["ws"], 1)
                    pe.wait_ge(co["vnew"], hg + 1)
                    for h in range(4):
                        M(bank[1][:, cols4(h)], SS[:, cols4(h)], QG[:, cols4(h)], start=True, stop=False)
                        ins = M(bank[1][:, cols4(h)], U[:, 1, cols4(h)], AT[:, 1, cols4(h)], start=False, stop=True)
                    ins.then_inc(co["o1"], 1)
                    for p in range(2):
                        pe.wait_ge(co["osq"], 2 * hg + p + 1)
                        M(bank[p and 6][:, :], mean_hd[:, :], sq[:, p, :], start=True, stop=True).then_inc(co["oss"], 1)
                project(G_GDN_OUT, co["olo"], 4)

            def latent_sum(nt, count):
                pe.wait_ge(am["latsq"], count)
                M(half(2, 0), ones[:, :], sq[:, 0, 0:T], start=True, stop=False)
                ins = M(half(2, 0), ones[:, :], sq[:, 0, T:2 * T], start=False, stop=nt == 2)
                if nt == 3:
                    ins = M(half(2, 0), ones[:, :], sq[:, 1, 0:T], start=False, stop=True)
                ins.then_inc(am["latss"], 1)

            def swaps(src, n, c0):
                w = src.shape[1] // n
                for c in range(n):
                    pe.wait_ge(am["gained"], c0 + c + 1)
                    M(swap_bank(n, c)[:, 0:w * T], mat[:, M_SWAP, :], src[:, c * w:(c + 1) * w, :], start=True, stop=True).then_inc(am["swap"], 1)

            def head_sums(first):
                p0 = 0 if first else 4
                for j in range(4):
                    p = p0 + j
                    pe.wait_ge(am["hsq"], p + 1)
                    if p >= 2:
                        pe.wait_ge(am["hstd"], p - 1)
                    M(bank[j % 2][:, :], ones[:, :], sq[:, j % 2, :], start=True, stop=False, skip_group_check=True)
                    for e in range(2):
                        ins = M(half(j % 2, e), mat[:, M_LOW + e, :], sqr[:, 0 if first else j, :], start=False, stop=True,
                                skip_group_check=True)
                    ins.then_inc(am["hss"], 1)

            def kv(n):
                g = G_KV
                pe.wait_ge(w_lo, g + 1)
                col_tile(half(0, 0), g % 2, 0, KD, hh, hl, (h_ready, 8 * n))
                col_tile(half(0, 1), g % 2, KD, KD, hh, hl).then_inc(w_used, 1)
                pe.wait_ge(w_lo, g + 2)
                col_tile(half(1, 0), (g + 1) % 2, 0, KD, hh, hl).then_inc(w_used, 1)
                latent_sum(KV_LORA_T, 1)
                pe.wait_ge(w_lo, g + 3)
                pe.wait_ge(am["latlo"], 2)
                pe.wait_ge(am["ropesq"], 1)
                for p in range(4):
                    if p >= 2:
                        pe.wait_ge(am["kev"], p - 1)
                    for e in range(2):
                        ins = col_tile(half(p % 2, e), g % 2, 2 * (2 * p + e), 2, lath, latl)
                    ins.then_inc(am["kraw"] if p < 3 else w_used, 1)
                swaps(lat[:, 2:3, :], 1, 0)
                pe.wait_ge(w_lo, g + 4)
                for b in range(2):
                    for c in range(2):
                        dst = bank[4 + 2 * b + c][:, :]
                        for k in range(2):
                            ht = slice(b * P, b * P + P)
                            w = slice(D * k + 512 * c, D * k + 512 * c + 512)
                            sl = (g + 3) % 2
                            M(dst, lath[:, k, ht], wh[:, sl, w], start=k == 0, stop=False)
                            M(dst, latl[:, k, ht], wh[:, sl, w], start=False, stop=False)
                            ins = M(dst, lath[:, k, ht], wl[:, sl, w], start=False, stop=k == 1)
                ins.then_inc(w_used, 1)
                pe.wait_ge(am["kev"], 4)
                head_sums(True)

            def mla(n, u0):
                g = G_MLA
                pe.wait_ge(w_lo, g + 1)
                col_tile(half(0, 0), g % 2, 0, KD, hh, hl, (h_ready, 8 * n))
                col_tile(half(0, 1), g % 2, KD, KD, hh, hl).then_inc(w_used, 1)
                ada_reduce(u0 - 1)
                pe.wait_ge(w_lo, g + 2)
                col_tile(half(1, 0), (g + 1) % 2, 0, KD, hh, hl).then_inc(w_used, 1)
                latent_sum(Q_LORA_T, 3)
                for p in range(6):
                    if p % 2 == 0:
                        pe.wait_ge(w_lo, g + 2 + p // 2 + 1)
                    if p == 0:
                        pe.wait_ge(am["latlo"], 5)
                    if p >= 2:
                        pe.wait_ge(am["qev"], p - 1)
                    for e in range(2):
                        ins = col_tile(half(p % 2, e), (g + 2 + p // 2) % 2, 3 * (2 * (p % 2) + e), 3, lath, latl)
                    ins.then_inc(w_used if p % 2 else am["qraw"], 1)
                    if p % 2:
                        ada_reduce(u0 + p // 2)
                swaps(qr[:, :, :], 2, 1)
                pe.wait_ge(am["qev"], 6)
                pe.wait_ge(am["ropesq"], 3)
                head_sums(False)
                pe.wait_ge(am["hn"], 8)
                for i in range(HEADS + 2):
                    if i < HEADS:
                        h, e, j = i, i % 2, i // 2
                        hp = slice(64 * (h % 2), 64 * (h % 2) + 64)
                        if h >= 2:
                            pe.wait_ge(am["exp"], h - 1)
                        for qb in range(2):
                            qs = slice(qb * P, qb * P + P)
                            dst = bank[e][:, qb * T:qb * T + P * (qb + 1)]
                            M(dst, qn[:, h, qs], kn[:, h, 0:P * (qb + 1)], start=True, stop=False)
                            ins = M(dst, qr[hp, j, qs], kr[hp, j, 0:P * (qb + 1)], start=False, stop=True)
                        ins.then_inc(am["s"], 1)
                    if 1 <= i <= HEADS:
                        h = i - 1
                        pe.wait_ge(am["p"], h + 1)
                        if h >= 2:
                            pe.wait_ge(am["pt"], h - 1)
                        for c in range(3):
                            ins = nc.tensor.transpose(bank[4 + h % 2][:, P * c:P * c + P], prb[:, h % 2, P * c:P * c + P], mat[:, M_ID, :])
                        ins.then_inc(am["turned"], 1)
                    if i >= 2:
                        h = i - 2
                        pe.wait_ge(am["pt"], h + 1)
                        if h >= 2:
                            pe.wait_ge(am["olo"], h - 1)
                        v = [vt[:, b, P * h:P * h + P] for b in range(2)]
                        dst = bank[6 + h % 2]
                        M(dst[:, 0:P], v[0], pt[:, h % 2, 0:P], start=True, stop=True)
                        M(dst[:, P:2 * P], v[0], pt[:, h % 2, P:2 * P], start=True, stop=False)
                        M(dst[:, P:2 * P], v[1], pt[:, h % 2, 2 * P:3 * P], start=False, stop=True).then_inc(am["o"], 1)
                project(G_MLA_OUT, am["olo"], HEADS, (u0 + 3, u0 + 4))
                ada_reduce(u0 + 5)

            pe.wait_ge(set_consts, 1)
            stats(0)
            for u in range(ADA_FIRST - 1):
                ada_reduce(u)
            ffn(0, 0, ADA_FIRST)
            stats(1)
            gdn(1, ADA_FIRST + 19)
            stats(2)
            ffn(1, 2, ADA_FIRST + 27)
            stats(3)
            kv(3)
            ffn(2, 4, ADA_FIRST + 46)
            stats(4)
            mla(5, ADA_FIRST + 65)
            stats(5)
            ffn(3, 6, None)


def square_consts():
    import numpy as np
    i = np.arange(P)
    out = np.zeros((P, M_COUNT, P), np.float32)
    row, colm = i[:, None], i[None, :]
    out[:, M_ID] = row == colm
    out[:, M_LE] = row <= colm
    out[:, M_GT] = row > colm
    out[:, M_ST] = row < colm
    out[:, M_SWAP] = row == (colm ^ 32)
    out[:, M_LOW] = row + 0 * colm < P // 2
    out[:, M_HIGH] = row + 0 * colm >= P // 2
    for lv in range(LEVELS):
        s = 1 << lv
        low = (row // (2 * s) == colm // (2 * s)) & (row // s % 2 == 1) & (colm // s % 2 == 0)
        out[:, M_LV + lv] = low
        if lv == 0:
            out[:, M_LVT] = low.T
    return out


def kernel(**inputs):
    import numpy as np
    import concourse.bacc as bacc
    from concourse.bass_utils import run_bass_kernel_spmd

    a = {k: np.asarray(v) for k, v in inputs.items()}
    f32 = np.float32

    def by_partition(v):
        v = v.reshape(v.shape[:-1] + (v.shape[-1] // P, P))
        return np.moveaxis(v, -1, 0).reshape(P, -1)

    def tiles(w):
        return w.reshape(w.shape[0] // P, P, w.shape[1] // P, P).transpose(2, 0, 1, 3)

    def granule(t, per=TILES):
        g = np.zeros((len(t) // per, P, TILES, P), f32)
        g[:, :, :per] = t.reshape(-1, per, P, P).transpose(0, 2, 1, 3)
        return g.reshape(-1, P, GW)

    def ffn(l, i):
        w = tiles(a["ffn_w_in"][l, i])
        both = np.stack([w[:FT], w[FT:]], 1)
        o = tiles(a["ffn_w_out"][l, i]).transpose(1, 0, 2, 3)
        return [granule(both.reshape(-1, P, P)), granule(o.reshape(-1, P, P))]

    def proj(w):
        return granule(tiles(w).transpose(1, 0, 2, 3).reshape(-1, P, P))

    gin = a["gdn_w_in"][0]
    dkv = a["mla_w_dkv"]
    rope = tiles(np.concatenate([dkv[:, 256:], dkv[:, 256:]], 1))[0]
    ukv = a["mla_w_ukv"].reshape(256, HEADS, 256)
    uv = ukv[:, :, P:].reshape(2, P, D).transpose(1, 0, 2).reshape(1, P, GW)
    uq = a["mla_w_uq"][0].reshape(Q_LORA_T * P, HEADS, QK_HEAD)
    uq_all = np.concatenate([uq[:, :, :P].reshape(-1, D), uq[:, :, P:].reshape(-1, D // 2)], 1)
    dq = tiles(a["mla_w_dq"][0])
    wstream = np.concatenate(
        ffn(0, 0) + [granule(tiles(gin[:, :4 * D]).reshape(-1, P, P)), proj(a["gdn_w_out"][0])] + ffn(0, 1)
        + [granule(tiles(dkv[:, :256]).reshape(-1, P, P)), granule(rope, KD),
           granule(tiles(np.ascontiguousarray(ukv[:, :, :P]).reshape(256, D)).reshape(-1, P, P)), uv] + ffn(1, 0)
        + [granule(dq[:2].reshape(-1, P, P)), granule(dq[2], KD), granule(tiles(uq_all).reshape(-1, P, P), 12),
           proj(a["mla_w_out"][0])] + ffn(1, 1))
    assert wstream.shape[0] == GRANULES

    def ada_units(w):
        return w.reshape(KD, P, -1, 256).transpose(2, 1, 0, 3)

    ada = np.concatenate([ada_units(a["ada_w"][0]), ada_units(a["kv_ada_w"]), ada_units(a["ada_w"][1])])
    ada_b = np.concatenate([by_partition(a["ada_b"][0]), by_partition(a["kv_ada_b"]), by_partition(a["ada_b"][1])], 1)
    half = 32
    freq = (f32(10000.0) ** (-np.arange(half, dtype=f32) / f32(half))).astype(f32)
    kg, qg = a["mla_k_norm_g"], a["mla_q_norm_g"][0]
    cols = np.zeros((P, C_COLS), f32)
    cols[:, C_NORM:C_NORM + 48] = by_partition(a["norm_g"])
    cols[:, C_KVN:C_KVN + 8] = by_partition(a["kv_norm_g"])
    cols[:, C_CONV:C_CONV + 96] = by_partition(a["gdn_conv_w"][0])
    cols[:, C_GDNN] = a["gdn_norm_g"][0]
    cols[:, C_KVL:C_KVL + 2] = by_partition(a["mla_kv_norm_g"])
    cols[:, C_QL:C_QL + 3] = by_partition(a["mla_q_lora_norm_g"])
    cols[:, C_KN], cols[:, C_KN + 1] = kg[:P], np.tile(kg[P:], 2)
    cols[:, C_QN], cols[:, C_QN + 1] = qg[:P], np.tile(qg[P:], 2)
    cols[:, C_FREQ] = np.tile(freq, 4)
    cols[:, C_SIGN] = np.tile(np.repeat(np.array([-1.0, 1.0], f32), half), 2)
    tok = np.broadcast_to(np.concatenate([a["gdn_dt_bias"][0], a["gdn_a_log"][0]]), (P, 16))
    arrays = {
        "x_in": a["x"][0].T.reshape(KD, P, T).transpose(1, 0, 2),
        "c_in": by_partition(a["c"][0]),
        "pos_in": np.broadcast_to(a["positions"][0], (P, T)),
        "wstream": wstream, "ada": ada, "ada_b": ada_b, "cols": cols, "tok": tok,
        "wba": gin[:, 4 * D:].reshape(KD, P, 16).transpose(1, 0, 2),
        "squares": square_consts(),
    }
    arrays = {k: np.ascontiguousarray(v) for k, v in arrays.items()}
    nc = bacc.Bacc("TRN2", target_bir_lowering=False, num_devices=1)
    args = [nc.dram_tensor(k, v.shape, mybir.dt.from_np(v.dtype), kind="ExternalInput").ap() for k, v in arrays.items()]
    args.append(nc.dram_tensor("y_out", (P, KD, T), F32, kind="ExternalOutput").ap())
    build(nc, *args)
    r = run_bass_kernel_spmd(nc, [arrays], core_ids=[0])
    y = r.results[0]["y_out"]
    return y.transpose(1, 0, 2).reshape(1, D, T).transpose(0, 2, 1)
```

```python
from contextlib import ExitStack

import concourse.bass as bass
from concourse import mybir

F32 = mybir.dt.float32
F32R = mybir.dt.float32r
I32 = mybir.dt.int32
ALU = mybir.AluOpType
ACT = mybir.ActivationFunctionType
AX = mybir.AxisListType.X

P = 128
D = 1024
T = 256
KD = D // P
DFF = 2816
FT = DFF // P
HEADS = 8
EPS = 1e-6
TILES = 16
GW = TILES * P
RAW = 4
FFN_IN, FFN_OUT = FT, FT // 2
GDN_IN, PROJ_OUT = 16, 4
G_FFN = [0, 53, 90, 132]
G_GDN = 33
G_GDN_OUT = G_GDN + GDN_IN
G_KV = 86
G_MLA = 123
G_MLA_OUT = 128
GRANULES = 165
ADA_UNITS = 80
STAGED = 8
U_FFN, U_GDN, U_KV, U_MLA = [9, 35, 53, 76], 25, 51, 69
BY_PE = STAGED // 2
POOL_GDN, POOL_MLA = 10, 5
LEVELS = 7
KV_LORA_T, Q_LORA_T = 2, 3
QK_HEAD = 192
NEG = -1e30
TWO_PI = 6.283185307179586
RND = 12582912.0


def mod_index(layer, j):
    return j if layer == 0 else 11 + j


C_NORM = 0
C_KVN = 48
C_CONV = 56
C_GDNN = C_CONV + 96
C_KVL = C_GDNN + 1
C_QL = C_KVL + 2
C_KN = C_QL + 3
C_QN = C_KN + 2
C_FREQ = C_QN + 2
C_SIGN = C_FREQ + 1
C_COLS = C_SIGN + 1

M_ID, M_LE, M_GT, M_ST, M_LVT, M_SWAP, M_LOW, M_HIGH, M_LV = range(9)
M_COUNT = M_LV + LEVELS


def build(nc, x_in, c_in, pos, wstream, ada, ada_b, cols, tok, wba_dram, squares, out):
    ctx = ExitStack()
    with ctx:
        base = [nc.sbuf_base + (-nc.sbuf_base) % 64]

        def at(name, shape, dtype, offset):
            return nc.alloc_sbuf_tensor_at(name, shape, dtype, offset=offset)

        def sb(name, shape, dtype=F32):
            n = 4
            for s in shape[1:]:
                n *= s
            t = at(name, shape, dtype, base[0])
            base[0] += n + (-n) % 64
            return t

        def sem(name):
            return ctx.enter_context(nc.semaphore(name))

        bank = [ctx.enter_context(nc.psum_tensor(f"bank{i}", [P, 512], F32)) for i in range(8)]

        raw = sb("w_raw", [P, RAW, GW])
        wh = sb("w_hi", [P, 2, GW], F32R)
        wl = sb("w_lo", [P, 2, GW], F32R)
        araw = sb("ada_raw", [P, 2, KD, 256])
        acc = sb("ada_acc", [P, 256])
        x = sb("x", [P, KD, T])
        hh = sb("h_hi", [P, KD, T], F32R)
        hl = sb("h_lo", [P, KD, T], F32R)
        mods = sb("mods", [P, 2 * ADA_UNITS])
        modb = sb("mod_bias", [P, 2 * ADA_UNITS])
        col = sb("feature_consts", [P, C_COLS])
        mat = sb("square_consts", [P, M_COUNT, P])
        ones = sb("ones", [P, P])
        mean_d = sb("mean_d", [P, P])
        mean_hd = sb("mean_hd", [P, P])
        epsc = sb("eps_consts", [P, 4])
        craw = sb("c_raw", [P, KD])
        cact = sb("c_act", [P, KD])
        gs = sb("gain_scale", [P, KD])
        gate = sb("gate", [P, KD])
        warm = sb("warm", [P, 4])
        t2 = sb("norm_t", [P, 4, T])
        sq = sb("sq", [P, 2, 2 * T])
        std = sb("std", [P, 2, 2 * T])
        hst = sb("head_stats", [P, 4, 2 * HEADS])
        rstd = sb("rstd", [P, T])
        silu = sb("ff_silu_out", [P, 2, T])
        hid = sb("ff_hid32", [P, 2, T])
        pacc, pmul = t2, hid
        eps_hd = sb("eps_head_sum", [P, P])
        cs = sb("cos_sin", [P, 2, T])
        shared = base[0]
        kn = sb("k_nope", [P, HEADS, T])
        kr = sb("k_rope", [P, HEADS // 2, T])
        vt = sb("v_tok", [P, 2, D])
        arena = base[0]
        angi = at("positions", [P, T], I32, shared)
        ang = at("angles", [P, 6, T], F32, shared + 4 * T)
        arow = at("ada_rows", [1, BY_PE * 256], F32, shared + 32 * T)
        stage = at("ada_staged", [P, STAGED - 2, KD, 256], F32, arena)
        fh = sb("ff_hid_hi", [P, FT, T], F32R)
        fl = sb("ff_hid_lo", [P, FT, T], F32R)
        ends = [base[0], arena + (STAGED - 2) * 4 * GW]

        base[0] = shared
        KDC = sb("k_dec", [P, 512])
        RK = sb("rhs_k", [P, 512])
        SS = at("state", [P, 512], F32, base[0] - 2048)
        QG = sb("q_g", [P, 512])
        WT = sb("w_t", [P, 512])
        TMP = sb("masked_cols", [P, 2, 512])
        AT = sb("attn_t", [P, 2, 512])
        LT = sb("lower_t", [P, 2, 512])
        assert base[0] <= arena
        spare = shared + 12 * 1024
        wba = at("wba", [P, KD, 16], F32, spare)
        wbah = at("wba_hi", [P, KD, 16], F32R, spare + 512)
        wbal = at("wba_lo", [P, KD, 16], F32R, spare + 1024)
        tokc = at("tok_consts", [P, 16], F32, spare + 1536)
        base[0] = arena
        qkv = sb("qkv", [P, 24, T])
        zs = sb("z_silu", [P, HEADS, T])
        bas = sb("ba_by_column", [16, T])
        sc = sb("gate_scalars", [P, 14, 2, 8])
        X = sb("inv", [P, 2, 512])
        O32 = at("o32", [P, 4, T], F32, base[0] - 4096)
        XT = sb("inv_t", [P, 2, 512])
        BS = at("beta_strict", [P, 2, 512], F32, base[0] - 4096)
        PS = sb("inv_p", [P, 2, 512])
        DC = at("decay_t", [P, 2, 512], F32, base[0] - 4096)
        RV = sb("rhs_v", [P, 2, 512])
        U = at("u", [P, 2, 512], F32, base[0] - 4096)
        ends.append(base[0])

        base[0] = arena
        lat = sb("lat", [P, 3, T])
        lath = sb("lat_hi", [P, 3, T], F32R)
        latl = sb("lat_lo", [P, 3, T], F32R)
        qn = sb("q_nope", [P, HEADS, T])
        qr = sb("q_rope", [P, HEADS // 2, T])
        rot = sb("rot_t", [P, 2 * T])
        sqr = sb("rope_sq", [P, HEADS // 2, T])
        prb = sb("probs", [P, 2, 384])
        pt = sb("probs_t", [P, 2, 384])
        st = sb("soft_stats", [P, 2, 8])
        ends.append(base[0])
        assert max(ends) <= nc.sbuf_usable_end, (ends, nc.sbuf_usable_end)

        w_landed = [sem(f"w_landed{i}") for i in range(RAW)]
        w_hi, w_lo, w_used = sem("w_hi"), sem("w_lo"), sem("w_used")
        ada_landed = [sem(f"ada_landed{i}") for i in range(2)]
        staged = [sem(f"ada_staged{i}") for i in range(STAGED)]
        pe_units, ada_rows, ada_cols = sem("ada_by_pe"), sem("ada_rows_sem"), sem("ada_cols")
        ada_pool, pool_red, pool_link = sem("ada_pool"), sem("pool_red"), sem("pool_link")
        ada_mac, ada_red, ada_done = sem("ada_mac"), sem("ada_red"), sem("ada_done")
        c_in_sem, squares_in = sem("c_in_sem"), sem("squares_in")
        consts_in, x_in_sem, set_consts = sem("consts_in"), sem("x_in"), sem("set_consts")
        c_ready = sem("c_ready")
        x_upd, y_done = sem("x_upd"), sem("y_done")
        sq_ready, ss_mm, std_ready = sem("sq_ready"), sem("ss_mm"), sem("std_ready")
        mod_t, hh_ready, h_ready = sem("mod_t"), sem("hh_ready"), sem("h_ready")
        ff_silu, ff_hid, ff_hi, ff_lo = sem("ff_silu"), sem("ff_hid"), sem("ff_hi"), sem("ff_lo")
        gc_first, gc_tap, gc_conv, gc_silu, gz_silu = (sem("gc_" + n) for n in ("first", "tap", "conv", "silu", "z"))
        ba_in, ba_hi, ba_lo, ba_done = sem("ba_in"), sem("ba_hi"), sem("ba_lo"), sem("ba_done")
        ba_sb, ba_turned = sem("ba_sb"), sem("ba_turned")
        dve_link, act_link = sem("dve_link"), sem("act_link")
        gt_act, gt_dve, gt_pe = sem("gt_act"), sem("gt_dve"), sem("gt_pe")
        l2_sq, l2_ss, l2_std = (sem("l2_" + n) for n in ("sq", "ss", "std"))
        co = {n: sem("co_" + n) for n in (
            "gm", "bm", "gq", "kq", "bs", "at", "qsq", "kvt", "dd", "decay", "lt", "turned", "tokd", "u", "uu", "state", "state_sb", "ws", "vnew",
            "o0", "o1", "osb", "osq", "oss", "ostd", "onorm", "ohi", "olo")}
        inv_x = [sem(f"inv_x{b}") for b in range(2)]
        inv_p = [sem(f"inv_p{b}") for b in range(2)]
        inv_ps = [sem(f"inv_ps{b}") for b in range(2)]
        inv_xp = [sem(f"inv_xp{b}") for b in range(2)]
        am = {n: sem("am_" + n) for n in (
            "angle", "sin", "latsq", "latss", "latstd", "latn", "lathi", "latlo", "kraw", "qraw", "vev", "gained",
            "swap", "ropesq", "hsq", "hss", "ropess", "hsum", "hstd", "hdiag", "hcast", "hn", "rotated", "s", "max",
            "exp", "p", "turned", "pt", "o", "ohi", "olo")}
        stored = sem("stored")

        out_stages = {"ffn0": 0, "gdn": 1, "ffn1": 2, "ffn2": 3, "mla": 4, "ffn3": 5}
        last_v = len(out_stages) - 1
        granules, norms = GRANULES, len(out_stages)

        def half(b, e):
            return bank[b][:, e * T:(e + 1) * T]

        def staged_unit(u):
            if u < STAGED - 2:
                return stage[:, u, :, :]
            return raw[:, u - STAGED + RAW, :].rearrange("p (k c) -> p k c", k=KD)

        def wide(ap, n):
            return ap.unsqueeze(1).to_broadcast([P, n, ap.shape[-1]])

        def swap_bank(n, c):
            return bank[2][:, T:2 * T] if n == 1 else bank[4 + c][:, :]

        def diagonal(j):
            return (sq if j < 2 else std)[:, j % 2, :]

        def pairs(ap):
            return ap.rearrange("p (e t) -> p e t", e=2)

        def heads4(ap):
            return ap.rearrange("p (h t) -> p h t", h=4)

        block = ctx.enter_context(nc.Block())

        @block.sync
        def _(sp):
            sp.dma_start(craw[:, :], c_in).then_inc(c_in_sem, 16)

            def stage_unit(u):
                sp.dma_start(staged_unit(u), ada[u]).then_inc(staged[u], 16)

            def first_granule(g):
                sp.dma_start(raw[:, g, :], wstream[g]).then_inc(w_landed[g], 16)

            stage_unit(0)
            stage_unit(1)
            sp.dma_start(angi[:, :], pos).then_inc(consts_in, 16)
            sp.dma_start(col[:, :], cols).then_inc(consts_in, 16)
            sp.dma_start(modb[:, :], ada_b).then_inc(consts_in, 16)
            sp.dma_start(x[:, :, :], x_in).then_inc(x_in_sem, 16)
            for u in range(2, 6):
                sp.wait_ge(staged[u - 2], 16)
                stage_unit(u)
            sp.wait_ge(staged[4], 16)
            stage_unit(6)
            sp.wait_ge(staged[5], 16)
            stage_unit(7)
            sp.wait_ge(staged[6], 16)
            first_granule(0)
            sp.wait_ge(staged[7], 16)
            first_granule(1)
            sp.wait_ge(ada_mac, BY_PE * KD)
            first_granule(2)
            sp.wait_ge(pe_units, 1)
            first_granule(3)
            sp.dma_start(mat[:, :, :], squares).then_inc(squares_in, 16)
            sp.dma_start(wba[:, :, :], wba_dram).then_inc(ba_in, 16)
            sp.dma_start(tokc[:, :], tok).then_inc(ba_in, 16)
            turns = (granules - RAW) // RAW
            with sp.Fori(0, turns) as i:
                for r in range(RAW):
                    sp.wait_ge(w_lo, i * RAW + (r + 1))
                    sp.dma_start(raw[:, r, :], wstream[i * RAW + (RAW + r)]).then_inc(w_landed[r], 16)
            for g in range(RAW + turns * RAW, granules):
                sp.wait_ge(w_lo, g - RAW + 1)
                sp.dma_start(raw[:, g % RAW, :], wstream[g]).then_inc(w_landed[g % RAW], 16)
            for m in range(KD):
                sp.wait_ge(x_upd, 8 * last_v + m + 1)
                sp.dma_start(out[:, m, :], x[:, m, :]).then_inc(stored, 16)
            sp.wait_ge(stored, 16 * KD)

        @block.gpsimd
        def _(pool):
            nc.gpsimd.memset(ones[:, :], 1.0)
            nc.gpsimd.memset(mean_d[:, :], 1.0 / D)
            nc.gpsimd.memset(mean_hd[:, :], 1.0 / P)
            nc.gpsimd.memset(epsc[:, 0:1], EPS)
            nc.gpsimd.memset(eps_hd[:, :], EPS * P)
            nc.gpsimd.memset(epsc[:, 1:2], EPS * EPS * P)
            nc.gpsimd.memset(epsc[:, 2:3], EPS * QK_HEAD)
            nc.gpsimd.memset(epsc[:, 3:4], 1.0).then_inc(set_consts, 1)
            pool.wait_ge(w_landed[0], 16)
            for u in range(2):
                pool.dma_start(araw[:, u, :, :], ada[STAGED + u]).then_inc(ada_landed[u], 16)

            def load(u, par, skip):
                pool.wait_ge(ada_mac, u * KD - (1 + skip) * KD)
                pool.dma_start(araw[:, par, :, :], ada[u]).then_inc(ada_landed[par], 16)

            def loads(u0, u1, skip):
                turns = (u1 - u0) // 2
                with pool.Fori(0, turns) as i:
                    for q in range(2):
                        load(i * 2 + (u0 + q), (u0 + q) % 2, skip)
                for u in range(u0 + 2 * turns, u1):
                    load(u, u % 2, skip)

            def unit(n, u):
                par, a = u % 2, n % 4
                pool.wait_ge(ada_landed[par], 16 * ((u - STAGED) // 2 + 1))
                if n >= 4:
                    pool.wait_ge(pool_red, n - 3)
                for k in range(KD):
                    if k == 0:
                        nc.gpsimd.tensor_scalar(pacc[:, a, :], araw[:, par, k, :], cact[:, k:k + 1], None, ALU.mult)
                    else:
                        nc.gpsimd.tensor_scalar(pmul[:, k % 2, :], araw[:, par, k, :], cact[:, k:k + 1], None, ALU.mult).then_inc(pool_link, 1)
                        pool.wait_ge(pool_link, (KD - 1) * n + k)
                        ins = nc.gpsimd.tensor_tensor(pacc[:, a, :], pacc[:, a, :], pmul[:, k % 2, :], ALU.add)
                ins.then_inc(ada_pool, 1)
                if u + 2 < ADA_UNITS:
                    pool.wait_ge(ada_pool, n + 1)
                    pool.dma_start(araw[:, par, :, :], ada[u + 2]).then_inc(ada_landed[par], 16)

            loads(STAGED + 2, U_GDN + 2, BY_PE)
            pool.wait_ge(h_ready, 2 * KD)
            for n in range(POOL_GDN):
                unit(n, U_GDN + n)
            loads(U_GDN + POOL_GDN + 2, U_MLA + 2, BY_PE + POOL_GDN)
            pool.wait_ge(h_ready, 6 * KD)
            for n in range(POOL_MLA):
                unit(POOL_GDN + n, U_MLA + n)
            loads(U_MLA + POOL_MLA + 2, ADA_UNITS, BY_PE + POOL_GDN + POOL_MLA)

        @block.scalar
        def _(act):
            A = nc.scalar.activation

            def split_hi(g, r, at_start=False):
                act.wait_ge(w_landed[r], (g - r) * 4 + 16)
                if not at_start:
                    act.wait_ge(w_used, g - 1)
                nc.scalar.copy(wh[:, r % 2, :], raw[:, r, :]).then_inc(w_hi, 1)

            def split_next(g, r):
                if isinstance(g, int) and g + 2 >= granules:
                    return
                split_hi(g + 2, (r + 2) % RAW)

            def linked(n, ins):
                ins.then_inc(act_link, 1)
                act.wait_ge(act_link, n)

            def stats(v, g_last=None):
                A(warm[:, 0:1], epsc[:, 3:4], ACT.Sqrt)
                for m in range(KD):
                    if v:
                        act.wait_ge(x_upd, 8 * (v - 1) + m + 1)
                    elif m == 0:
                        act.wait_ge(x_in_sem, 16)
                    if 8 * v + m >= 4:
                        act.wait_ge(ss_mm, 8 * v + m - 3)
                    A(sq[:, m // 2 % 2, m % 2 * T:m % 2 * T + T], x[:, m, :], ACT.Square).then_inc(sq_ready, 1)
                act.wait_ge(ss_mm, 8 * v + KD)
                A(std[:, 0, 0:T], half(2, 0), ACT.Sqrt, bias=epsc[:, 0:1]).then_inc(std_ready, 1)
                if g_last is not None:
                    split_next(g_last, g_last % RAW)

            def modulate(n, vec):
                if n == 4:
                    act.wait_ge(w_used, G_KV + 2)
                for m in range(KD):
                    act.wait_ge(mod_t, 8 * n + m + 1)
                    A(hh[:, m, :], t2[:, m % 4, :], ACT.Identity, bias=mods[:, 8 * vec + m:8 * vec + m + 1]).then_inc(hh_ready, 1)

            def ffn_in_step(f, g, j, r, par):
                act.wait_ge(w_used, g + 1)
                A(silu[:, par, :], half(par, 0), ACT.Silu).then_inc(ff_silu, 1)
                split_next(g, r)
                act.wait_ge(ff_hid, j + (22 * f + 1))
                nc.scalar.copy(fh[:, j, :], hid[:, par, :]).then_inc(ff_hi, 1)

            def ffn(f):
                g0 = G_FFN[f]
                for j in (0, 1):
                    ffn_in_step(f, g0 + j, j, (g0 + j) % RAW, j)
                with act.Fori(0, 5) as i:
                    for q in range(4):
                        ffn_in_step(f, i * 4 + (g0 + 2 + q), i * 4 + (2 + q), (g0 + 2 + q) % RAW, q % 2)
                g1 = g0 + FFN_IN
                turns = 1 if g1 + FFN_OUT == granules else 2
                split_next(g1, g1 % RAW)
                with act.Fori(0, turns) as i:
                    for q in range(4):
                        split_next(i * 4 + (g1 + 1 + q), (g1 + 1 + q) % RAW)
                for o in range(1 + 4 * turns, FFN_OUT - 1):
                    split_next(g1 + o, (g1 + o) % RAW)

            def gdn():
                def tile_pair(g, r, n, t0, par):
                    act.wait_ge(w_used, g + 1)
                    for e in range(2):
                        act.wait_ge(gc_silu, t0 + (e - 1))
                        A(silu[:, e, :], half(par, e), ACT.Identity,
                          scale=col[:, bass.ds(t0 + (C_CONV + 72 + e), 1)]).then_inc(gc_first, 1)
                    split_next(g, r)
                    for e in range(2):
                        act.wait_ge(gc_conv, t0 + (e + 1))
                        A(qkv[:, t0 + e, :], silu[:, e, :], ACT.Silu).then_inc(gc_silu, 1)

                def first_pair():
                    g = G_GDN
                    act.wait_ge(w_used, g + 1)
                    for e in range(2):
                        A(silu[:, e, :], half(0, e), ACT.Identity,
                          scale=col[:, C_CONV + 72 + e:C_CONV + 73 + e]).then_inc(gc_first, 1)
                    split_next(g, g % RAW)
                    for e in range(2):
                        act.wait_ge(gc_conv, e + 1)
                        A(qkv[:, e, :], silu[:, e, :], ACT.Silu).then_inc(gc_silu, 1)

                first_pair()
                for n in range(1, 4):
                    tile_pair(G_GDN + n, (G_GDN + n) % RAW, n, 2 * n, n % 2)
                with act.Fori(0, 2) as i:
                    for n in range(4, 8):
                        tile_pair(i * 4 + (G_GDN + n), (G_GDN + n) % RAW, n, i * 8 + 2 * n, n % 2)
                act.wait_ge(gt_dve, 1)
                linked(1, A(sc[:, 9, :, :], sc[:, 6, :, :], ACT.Abs))
                A(sc[:, 8, :, :], sc[:, 7, :, :], ACT.Exp, scale=-1.0)
                linked(2, A(sc[:, 10, :, :], sc[:, 9, :, :], ACT.Exp, scale=-1.0))
                A(sc[:, 12, 0, :], tokc[:, 8:16], ACT.Exp)
                A(sc[:, 11, :, :], sc[:, 10, :, :], ACT.Ln, bias=epsc[:, 3:4]).then_inc(gt_act, 1)
                for n in range(12, 16):
                    g = G_GDN + n
                    p = n - 12
                    if p >= 2:
                        act.wait_ge(l2_ss, p - 1)
                    A(pairs(sq[:, p % 2, :]), qkv[:, 8 + 2 * p:10 + 2 * p, :], ACT.Square).then_inc(l2_sq, 1)
                    act.wait_ge(w_used, g + 1)
                    z0 = 2 * (n - 12)
                    A(zs[:, z0:z0 + 2, :], pairs(bank[n % 2][:, :]), ACT.Silu).then_inc(gz_silu, 1)
                    split_next(g, g % RAW)
                act.wait_ge(gt_pe, 1)
                A(sc[:, 2, :, :], bank[2][:, 32:48].rearrange("p (b h) -> p b h", b=2), ACT.Copy)
                A(sc[:, 3, :, :], bank[2][:, 32:48].rearrange("p (b h) -> p b h", b=2), ACT.Exp)
                A(sc[:, 4, :, :], bank[2][:, 48:64].rearrange("p (b h) -> p b h", b=2), ACT.Exp).then_inc(gt_act, 1)
                act.wait_ge(l2_ss, 4)
                A(sc[:, 6, :, :], bank[2][:, 64:80].rearrange("p (b h) -> p b h", b=2), ACT.Sqrt, bias=epsc[:, 0:1]).then_inc(l2_std, 1)
                A(warm[:, 0:1], epsc[:, 3:4], ACT.Exp)
                for hg in range(2):
                    for b in range(2):
                        s = 2 * hg + b
                        act.wait_ge(co["dd"], s + 1)
                        A(DC[:, b, :], DC[:, b, :], ACT.Exp)
                        if b:
                            A(QG[:, :], bank[6 + b][:, :], ACT.Exp)
                        A(warm[:, 2:3], epsc[:, 3:4], ACT.Copy).then_inc(co["decay"], 1)
                        act.wait_ge(co["decay"], s + 1)
                    for b in range(2):
                        act.wait_ge(co["kvt"], 2 * hg + b + 1)
                        dst, c = (KDC, 4) if b == 0 else (RK, 5)
                        for h in range(4):
                            hc, hx = slice(P * h, P * h + P), 4 * hg + h
                            A(RV[:, b, hc], bank[6 + b][:, hc], ACT.Identity, scale=sc[:, 0, b, hx:hx + 1])
                            ins = A(dst[:, hc], bank[4 + b][:, hc], ACT.Identity, scale=sc[:, c, b, hx:hx + 1])
                        ins.then_inc(co["tokd"], 1)
                    act.wait_ge(co["kq"], 2 * hg + 2)
                    A(TMP[:, :, :].rearrange("p c (e t) -> p (c e) t", e=2), qkv[:, 4 * hg:4 * hg + 4, :], ACT.Square).then_inc(co["qsq"], 1)
                    for b in range(2):
                        act.wait_ge(co["o0" if b == 0 else "o1"], hg + 1)
                        A(O32[:, :, b * P:(b + 1) * P], heads4(bank[(4, 1)[b]][:, :]), ACT.Copy).then_inc(co["osb"], 1)
                    act.wait_ge(co["osb"], 2 * hg + 2)
                    for p in range(2):
                        q = 2 * hg + p
                        A(pairs(sq[:, p, :]), O32[:, 2 * p:2 * p + 2, :], ACT.Square).then_inc(co["osq"], 1)
                    for p in range(2):
                        q = 2 * hg + p
                        act.wait_ge(co["oss"], q + 1)
                        A(std[:, p, :], bank[5 + 2 * p][:, :], ACT.Ln, bias=epsc[:, 1:2]).then_inc(act_link, 1)
                    for p in range(2):
                        act.wait_ge(act_link, 3 + 2 * hg + p)
                        A(std[:, p, :], std[:, p, :], ACT.Exp, scale=-0.5).then_inc(co["ostd"], 1)
                    for p in range(2):
                        q = 2 * hg + p
                        act.wait_ge(co["onorm"], q + 1)
                        A(hh[:, 2 * q:2 * q + 2, :], O32[:, 2 * p:2 * p + 2, :], ACT.Copy).then_inc(co["ohi"], 1)
                for g in range(G_GDN_OUT, G_GDN_OUT + PROJ_OUT - 1):
                    split_next(g, g % RAW)

            def latent(nt, first, root_scale):
                act.wait_ge(am["latss"], 1 if first else 2)
                A(std[:, 0, 0:T], half(2, 0), ACT.Sqrt, bias=epsc[:, 0:1], scale=root_scale).then_inc(am["latstd"], 1)
                c0, i0 = (C_KVL, 0) if first else (C_QL, 2)
                for i in range(nt):
                    act.wait_ge(am["latn"], i0 + i + 1)
                    A(lath[:, i, :], lat[:, i, :], ACT.Identity, scale=col[:, c0 + i:c0 + i + 1]).then_inc(am["lathi"], 1)

            def head_squares(p, n):
                if n >= 2:
                    act.wait_ge(am["hss"], n - 1)
                A(sq[:, p % 2, :], bank[p % 2][:, :], ACT.Square).then_inc(am["hsq"], 1)

            def head_root(n, scale, bias):
                act.wait_ge(am["hsum"], n)
                A(hst[:, 1, :], hst[:, 0, :], ACT.Sqrt, bias=bias, scale=scale).then_inc(am["hstd"], 1)

            def kv():
                g = G_KV
                act.wait_ge(w_used, g + 1)
                A(lat[:, 0:2, :], pairs(bank[0][:, :]), ACT.Copy)
                A(sq[:, 0, :], bank[0][:, :], ACT.Square).then_inc(am["latsq"], 1)
                split_next(g, g % RAW)
                act.wait_ge(w_used, g + 2)
                A(lat[:, 2, :], half(1, 0), ACT.Copy)
                A(sqr[:, 0, :], half(1, 0), ACT.Square).then_inc(am["ropesq"], 1)
                split_next(g + 1, (g + 1) % RAW)
                latent(KV_LORA_T, True, 1.0 / (KV_LORA_T * P))
                for p in range(4):
                    if p < 3:
                        act.wait_ge(am["kraw"], p + 1)
                    else:
                        act.wait_ge(w_used, g + 3)
                    A(kn[:, 2 * p:2 * p + 2, :], pairs(bank[p % 2][:, :]), ACT.Copy)
                    head_squares(p, p)
                split_next(g + 2, (g + 2) % RAW)
                head_root(1, 1.0 / QK_HEAD, epsc[:, 0:1])
                act.wait_ge(w_used, g + 4)
                for b in range(2):
                    for c in range(2):
                        A(vt[:, b, 512 * c:512 * c + 512], bank[4 + 2 * b + c][:, :], ACT.Copy).then_inc(am["vev"], 1)
                split_next(g + 3, (g + 3) % RAW)

            def mla():
                g = G_MLA
                act.wait_ge(w_used, g + 1)
                A(lat[:, 0:2, :], pairs(bank[0][:, :]), ACT.Copy)
                A(sq[:, 0, :], bank[0][:, :], ACT.Square).then_inc(am["latsq"], 1)
                split_next(g, g % RAW)
                act.wait_ge(w_used, g + 2)
                A(lat[:, 2, :], half(1, 0), ACT.Copy)
                A(sq[:, 1, 0:T], half(1, 0), ACT.Square).then_inc(am["latsq"], 1)
                split_next(g + 1, (g + 1) % RAW)
                latent(Q_LORA_T, False, 1.0 / (Q_LORA_T * P))
                for p in range(6):
                    if p % 2 == 0:
                        act.wait_ge(am["qraw"], p // 2 + 1)
                    else:
                        act.wait_ge(w_used, g + 2 + p // 2 + 1)
                    dst = qn[:, 2 * p:2 * p + 2, :] if p < 4 else qr[:, 2 * p - 8:2 * p - 6, :]
                    gain = col[:, C_QN:C_QN + 1] if p < 4 else col[:, C_QN + 1:C_QN + 2]
                    A(dst, pairs(bank[p % 2][:, :]), ACT.Identity, scale=gain)
                    if p < 4:
                        head_squares(p, 4 + p)
                    else:
                        A(sqr[:, 2 * p - 8:2 * p - 6, :], pairs(bank[p % 2][:, :]), ACT.Square).then_inc(am["ropesq"], 1)
                    if p % 2:
                        split_next(g + 2 + p // 2, (g + 2 + p // 2) % RAW)
                head_root(2, 1.0, epsc[:, 2:3])
                A(warm[:, 3:4], epsc[:, 3:4], ACT.Exp)
                for i in range(HEADS + 3):
                    if 2 <= i < HEADS + 2:
                        h = i - 2
                        act.wait_ge(am["turned"], h + 1)
                        A(pt[:, h % 2, :], bank[4 + h % 2][:, 0:384], ACT.Copy).then_inc(am["pt"], 1)
                    if i < HEADS:
                        act.wait_ge(am["max"], i + 1)
                        e = i % 2
                        A(prb[:, e, 0:P], bank[e][:, 0:P], ACT.Exp, bias=st[:, e, 6:7],
                          scale=hst[:, 3, 2 * i:2 * i + 1], accum_out=st[:, e, 2:3])
                        A(prb[:, e, P:P + T], bank[e][:, T:2 * T], ACT.Exp, bias=st[:, e, 7:8],
                          scale=hst[:, 3, 2 * i + 1:2 * i + 2], accum_out=st[:, e, 3:4]).then_inc(am["exp"], 1)
                    if i >= 3:
                        h = i - 3
                        act.wait_ge(am["o"], h + 1)
                        A(hh[:, h, :], half(6 + h % 2, 0), ACT.Copy).then_inc(am["ohi"], 1)
                for g in range(G_MLA_OUT, G_MLA_OUT + PROJ_OUT - 1):
                    split_next(g, g % RAW)

            act.wait_ge(c_in_sem, 16)
            A(cact[:, :], craw[:, :], ACT.Silu).then_inc(c_ready, 1)
            act.wait_ge(set_consts, 1)
            stats(0)
            act.wait_ge(am["angle"], 1)
            A(cs[:, :, :], ang[:, 4:6, :], ACT.Sin).then_inc(am["sin"], 1)
            A(warm[:, 1:2], epsc[:, 3:4], ACT.Silu)
            split_hi(0, 0, True)
            act.wait_ge(pe_units, 1)
            for i in range(2):
                ins = A(arow[0:1, 2 * T * i:2 * T * i + 2 * T], bank[i][0:1, :], ACT.Copy)
            ins.then_inc(ada_rows, 1)
            modulate(0, mod_index(0, 0))
            split_hi(1, 1, True)
            ffn(0)
            act.wait_ge(ba_in, 32)
            nc.scalar.copy(wbah[:, :, :], wba[:, :, :]).then_inc(ba_hi, 1)
            stats(1, G_GDN - 1)
            modulate(1, mod_index(0, 3))
            A(warm[:, 1:2], epsc[:, 3:4], ACT.Silu)
            gdn()
            stats(2, G_FFN[1] - 1)
            modulate(2, mod_index(0, 6))
            A(warm[:, 1:2], epsc[:, 3:4], ACT.Silu)
            ffn(1)
            stats(3, G_KV - 1)
            modulate(3, 9)
            kv()
            modulate(4, mod_index(1, 0))
            ffn(2)
            stats(4, G_MLA - 1)
            modulate(5, mod_index(1, 3))
            mla()
            stats(5, G_FFN[3] - 1)
            modulate(6, mod_index(1, 6))
            A(warm[:, 1:2], epsc[:, 3:4], ACT.Silu)
            ffn(3)

        @block.vector
        def _(dve):
            V = nc.vector
            links = [0]
            skip = [BY_PE]

            def link(ins):
                links[0] += 1
                ins.then_inc(dve_link, 1)
                dve.wait_ge(dve_link, links[0])

            def split_lo(g, r):
                dve.wait_ge(w_hi, g + 1)
                V.tensor_tensor(wl[:, r % 2, :], raw[:, r, :], wh[:, r % 2, :].bitcast(F32), ALU.subtract).then_inc(w_lo, 1)

            def split_next(g, r):
                if isinstance(g, int) and g + 2 >= granules:
                    return
                split_lo(g + 2, (r + 2) % RAW)

            def ada_finish(u):
                dve.wait_ge(ada_red, u - skip[0])
                V.tensor_tensor(mods[:, bass.ds(u * 2 - 2, 2)], bank[3][:, 0:2], modb[:, bass.ds(u * 2 - 2, 2)],
                                ALU.add).then_inc(ada_done, 1)

            def mac(k, src, count):
                if k == 0:
                    V.tensor_scalar(acc[:, :], src, cact[:, 0:1], None, ALU.mult).then_inc(ada_mac, 1)
                else:
                    dve.wait_ge(ada_mac, count)
                    V.scalar_tensor_tensor(out=acc[:, :], in0=src, scalar=cact[:, k:k + 1], in1=acc[:, :],
                                           op0=ALU.mult, op1=ALU.add).then_inc(ada_mac, 1)

            def ada_step(u, par, which=None, finish=True):
                if which != 1:
                    if finish:
                        ada_finish(u)
                    dve.wait_ge(ada_landed[par], u * 8 - (8 * (STAGED - 2) + 8 * par))
                ks = range(KD) if which is None else range(KD // 2 * which, KD // 2 * which + KD // 2)
                for k in ks:
                    mac(k, araw[:, par, k, :], u * KD + (k - skip[0] * KD))

            def pool_columns(n0, count, u):
                dve.wait_ge(pool_red, n0 + count)
                link(V.tensor_tensor(mods[:, 2 * u:2 * (u + count)], bank[3][:, 0:2 * count], modb[:, 2 * u:2 * (u + count)], ALU.add))
                skip[0] += count

            def ada_staged(u):
                n = u // 2
                if n:
                    dve.wait_ge(ada_red, n)
                    V.tensor_tensor(mods[:, 2 * u - 4:2 * u - 2], bank[3][:, 0:2], modb[:, 2 * u - 4:2 * u - 2],
                                    ALU.add).then_inc(ada_done, 1)
                if u == STAGED:
                    return
                dve.wait_ge(staged[u], 16)
                for k in range(KD):
                    mac(k, staged_unit(u)[:, k, :], n * KD + k)

            def residual(stage, vec, factor, g_last):
                s = out_stages[stage]
                dve.wait_ge(ada_done, 4 * (vec + 1) - skip[0])
                link(V.tensor_scalar(gate[:, :], mods[:, 8 * vec:8 * vec + 8], factor, None, ALU.mult))
                for m in range(KD):
                    if m % 2 == 0 and m < KD - 2:
                        dve.wait_ge(y_done, 3 * s + m // 2 + 1)
                    elif m == KD - 2:
                        dve.wait_ge(w_used, g_last + 1)
                    V.scalar_tensor_tensor(out=x[:, m, :], in0=half(4 + m // 2, m % 2), scalar=gate[:, m:m + 1],
                                           in1=x[:, m, :], op0=ALU.mult, op1=ALU.add).then_inc(x_upd, 1)

            def gains(vec, c0):
                dve.wait_ge(ada_done, 4 * (vec + 2) - skip[0])
                link(V.scalar_tensor_tensor(out=gs[:, :], in0=mods[:, 8 * vec + 8:8 * vec + 16], scalar=1.0,
                                            in1=col[:, c0:c0 + 8], op0=ALU.add, op1=ALU.mult))

            def norm(v):
                dve.wait_ge(std_ready, v + 1)
                link(V.reciprocal(rstd[:, :], std[:, 0, 0:T]))

            def modulate(n, vec):
                if n == 4:
                    dve.wait_ge(w_used, G_KV + 2)
                for m in range(KD + 1):
                    if m < KD:
                        if 8 * n + m >= 4:
                            dve.wait_ge(h_ready, 8 * n + m - 3)
                        V.scalar_tensor_tensor(out=t2[:, m % 4, :], in0=x[:, m, :], scalar=gs[:, m:m + 1], in1=rstd[:, :],
                                               op0=ALU.mult, op1=ALU.mult).then_inc(mod_t, 1)
                    if m:
                        dve.wait_ge(hh_ready, 8 * n + m)
                        s = 8 * vec + m - 1
                        V.scalar_tensor_tensor(out=hl[:, m - 1, :], in0=t2[:, (m - 1) % 4, :], scalar=mods[:, s:s + 1],
                                               in1=hh[:, m - 1, :].bitcast(F32), op0=ALU.add, op1=ALU.subtract).then_inc(h_ready, 1)

            def ffn_in_step(f, g, j, r, par, unit=None):
                dve.wait_ge(ff_silu, j + (22 * f + 1))
                V.tensor_tensor(hid[:, par, :], silu[:, par, :], half(par, 1), ALU.mult).then_inc(ff_hid, 1)
                if unit is not None:
                    ada_step(*unit)
                split_next(g, r)
                dve.wait_ge(ff_hi, j + (22 * f + 1))
                V.tensor_tensor(fl[:, j, :], hid[:, par, :], fh[:, j, :].bitcast(F32), ALU.subtract).then_inc(ff_lo, 1)

            def ffn(f):
                g0, u0, last = G_FFN[f], U_FFN[f], f == 3
                for j in (0, 1):
                    ffn_in_step(f, g0 + j, j, (g0 + j) % RAW, j, (u0, u0 % 2, j, f == 0) if f != 2 else None)
                    if f == 2:
                        key_norm(2 * j)
                        key_norm(2 * j + 1)
                with dve.Fori(0, 5) as i:
                    for q in range(4):
                        u = u0 + 1 + q // 2
                        unit = None if last else (i * 2 + u, u % 2, q % 2)
                        ffn_in_step(f, i * 4 + (g0 + 2 + q), i * 4 + (2 + q), (g0 + 2 + q) % RAW, q % 2, unit)
                g1 = g0 + FFN_IN
                turns = 1 if last else 2
                u1 = u0 + 1 if last else u0 + 11
                split_next(g1, g1 % RAW)
                with dve.Fori(0, turns) as i:
                    for q in range(4):
                        u = u1 + q // 2
                        ada_step(i * 2 + u, u % 2, q % 2)
                        split_next(i * 4 + (g1 + 1 + q), (g1 + 1 + q) % RAW)
                u2, o1 = u1 + 2 * turns, 1 + 4 * turns
                for o in range(o1, FFN_OUT):
                    if o < o1 + 2:
                        ada_step(u2, u2 % 2, o - o1)
                    if last and o == o1 + 3:
                        ada_finish(u2 + 1)
                    if o < FFN_OUT - 1:
                        split_next(g1 + o, (g1 + o) % RAW)

            def conv(t0, par):
                dve.wait_ge(gc_first, t0 + 2)
                for d in range(1, 4):
                    for e in range(2):
                        if d > 1:
                            dve.wait_ge(gc_tap, t0 * 2 + (2 * d - 3 + e))
                        V.scalar_tensor_tensor(out=silu[:, e, d:T], in0=bank[par][:, e * T:(e + 1) * T - d],
                                               scalar=col[:, bass.ds(t0 + (C_CONV + 24 * (3 - d) + e), 1)], in1=silu[:, e, d:T],
                                               op0=ALU.mult, op1=ALU.add).then_inc(gc_tap if d < 3 else gc_conv, 1)

            def masked_decay(hg, b):
                gcol = sc[:, 1, b, 4 * hg:4 * hg + 4].unsqueeze(2).to_broadcast([P, 4, P])
                V.tensor_tensor(heads4(TMP[:, 0, :]), wide(mat[:, M_LE, :], 4), gcol, ALU.mult).then_inc(co["gm"], 1)

            def masked_strength(hg, b):
                bcol = sc[:, 8, b, 4 * hg:4 * hg + 4].unsqueeze(2).to_broadcast([P, 4, P])
                V.tensor_tensor(heads4(TMP[:, 1, :]), wide(mat[:, M_ID, :], 4), bcol, ALU.mult).then_inc(co["bm"], 1)

            def gdn():
                dve.wait_ge(squares_in, 16)

                def tile_pair(g, r, t0, par):
                    conv(t0, par)
                    split_next(g, r)

                for n in range(4):
                    g = G_GDN + n
                    tile_pair(g, g % RAW, 2 * n, n % 2)
                    if n == 0:
                        ada_finish(U_GDN)
                        dve.wait_ge(ba_done, 1)
                        V.tensor_copy(bas[:, :], bank[2][0:16, 0:T]).then_inc(ba_sb, 1)
                with dve.Fori(0, 2) as i:
                    for n in range(4, 8):
                        tile_pair(i * 4 + (G_GDN + n), (G_GDN + n) % RAW, i * 8 + 2 * n, n % 2)
                dve.wait_ge(ba_turned, 1)
                z16 = bank[2][:, T:T + 32].rearrange("p (b c) -> p b c", b=2)
                V.tensor_tensor(sc[:, 6, :, :], z16[:, :, 8:16], wide(tokc[:, 0:8], 2), ALU.add)
                V.tensor_copy(sc[:, 7, :, :], z16[:, :, 0:8]).then_inc(gt_dve, 1)
                dve.wait_ge(gt_act, 1)
                link(V.tensor_scalar(sc[:, 13, :, :], sc[:, 8, :, :], 1.0, None, ALU.add))
                V.reciprocal(sc[:, 0, :, :], sc[:, 13, :, :])
                link(V.scalar_tensor_tensor(out=sc[:, 5, :, :], in0=sc[:, 6, :, :], scalar=0.0, in1=sc[:, 11, :, :],
                                            op0=ALU.max, op1=ALU.add))
                V.scalar_tensor_tensor(out=sc[:, 1, :, :], in0=sc[:, 5, :, :], scalar=-1.0, in1=wide(sc[:, 12, 0, :], 2),
                                       op0=ALU.mult, op1=ALU.mult).then_inc(gt_dve, 1)
                for n in range(12, 16):
                    g = G_GDN + n
                    split_next(g, g % RAW)
                dve.wait_ge(gt_dve, 2)
                masked_decay(0, 0)
                dve.wait_ge(gt_act, 2)
                dve.wait_ge(l2_std, 1)
                link(V.reciprocal(sc[:, 7, :, :], sc[:, 6, :, :]))
                link(V.tensor_tensor(sc[:, 8, :, :], sc[:, 0, :, :], sc[:, 7, :, :], ALU.mult))
                V.tensor_tensor(sc[:, 5, :, :], sc[:, 8, :, :], sc[:, 3, :, :], ALU.mult)
                link(V.tensor_tensor(sc[:, 4, :, :], sc[:, 4, :, :], sc[:, 7, :, :], ALU.mult))
                masked_strength(0, 0)
                for hg in range(2):
                    hs = slice(4 * hg, 4 * hg + 4)
                    for b in range(2):
                        s = 2 * hg + b
                        dve.wait_ge(co["gq"], s + 1)
                        for h in range(4):
                            ins = V.tensor_scalar(DC[:, b, P * h:P * h + P], bank[6 + b][:, P * h:P * h + P],
                                                  sc[:, 2, b, 4 * hg + h:4 * hg + h + 1], 0.0, ALU.subtract, ALU.min)
                        ins.then_inc(co["dd"], 1)
                        dve.wait_ge(co["kq"], s + 1)
                        if b == 0:
                            masked_decay(hg, 1)
                            masked_strength(hg, 1)
                        V.tensor_tensor(heads4(BS[:, b, :]), heads4(bank[2][:, :]), wide(mat[:, M_ST, :], 4), ALU.mult).then_inc(co["bs"], 1)
                    for b in range(2):
                        s = 2 * hg + b
                        dve.wait_ge(co["decay"], s + 1)
                        for h in range(4):
                            hc = slice(P * h, P * h + P)
                            ins = V.scalar_tensor_tensor(out=DC[:, b, hc], in0=DC[:, b, hc], scalar=sc[:, 7, b, 4 * hg + h:4 * hg + h + 1],
                                                         in1=mat[:, M_LE, :], op0=ALU.mult, op1=ALU.mult)
                        link(ins)
                        link(V.tensor_tensor(LT[:, b, :], bank[b][:, :], DC[:, b, :], ALU.mult))
                        V.tensor_tensor(LT[:, b, :], LT[:, b, :], BS[:, b, :], ALU.mult).then_inc(co["lt"], 1)
                        V.tensor_tensor(AT[:, b, :], bank[4 + b][:, :], DC[:, b, :], ALU.mult).then_inc(co["at"], 1)
                        if b:
                            V.tensor_tensor(heads4(QG[:, :]), heads4(QG[:, :]), qkv[:, hs, b * P:(b + 1) * P], ALU.mult)
                    for b in range(2):
                        s = 2 * hg + b
                        dve.wait_ge(co["turned"], s + 1)
                        V.tensor_tensor(heads4(X[:, b, :]), heads4(bank[b][:, :]), wide(mat[:, M_LV, :], 4), ALU.mult)
                        link(V.tensor_tensor(heads4(XT[:, b, :]), heads4(LT[:, b, :]), wide(mat[:, M_LVT, :], 4), ALU.mult))
                        V.tensor_tensor(heads4(X[:, b, :]), wide(mat[:, M_ID, :], 4), heads4(X[:, b, :]), ALU.subtract)
                        V.tensor_tensor(heads4(XT[:, b, :]), wide(mat[:, M_ID, :], 4), heads4(XT[:, b, :]), ALU.subtract).then_inc(inv_x[b], 1)

                    def level(lv, n):
                        for b in range(2):
                            dve.wait_ge(inv_p[b], n)
                            V.tensor_tensor(heads4(PS[:, b, :]), heads4(bank[b][:, :]),
                                            mat[:, bass.ds(lv + M_LV, 1), :].to_broadcast([P, 4, P]), ALU.mult).then_inc(inv_ps[b], 1)
                        for b in range(2):
                            dve.wait_ge(inv_xp[b], n)
                            V.tensor_tensor(X[:, b, :], X[:, b, :], bank[4 + b][:, :], ALU.subtract)
                            V.tensor_tensor(XT[:, b, :], XT[:, b, :], bank[6 + b][:, :], ALU.subtract).then_inc(inv_x[b], 1)

                    with dve.Fori(1, LEVELS - 1) as lv:
                        level(lv, lv + hg * 6)
                    n = 6 + 6 * hg
                    for b in range(2):
                        dve.wait_ge(inv_p[b], n)
                        V.tensor_tensor(heads4(PS[:, b, :]), heads4(bank[b][:, :]), wide(mat[:, M_LV + LEVELS - 1, :], 4),
                                        ALU.mult).then_inc(inv_ps[b], 1)
                    for b in range(2):
                        dve.wait_ge(inv_xp[b], n)
                        V.tensor_tensor(XT[:, b, :], XT[:, b, :], bank[6 + b][:, :], ALU.subtract).then_inc(inv_x[b], 1)
                    for b in range(2):
                        s = 2 * hg + b
                        dve.wait_ge(co["u"], s + 1)
                        if b:
                            V.tensor_copy(WT[:, :], bank[4 + b][:, :])
                        V.tensor_copy(U[:, b, :], bank[b][:, :]).then_inc(co["uu"], 1)
                    dve.wait_ge(co["state"], hg + 1)
                    V.tensor_copy(SS[:, :], bank[6][:, :]).then_inc(co["state_sb"], 1)
                    dve.wait_ge(co["ws"], hg + 1)
                    V.tensor_tensor(U[:, 1, :], U[:, 1, :], bank[7][:, :], ALU.subtract).then_inc(co["vnew"], 1)
                    if hg == 0:
                        dve.wait_ge(co["oss"], 2)
                        masked_decay(1, 0)
                        masked_strength(1, 0)
                    for p in range(2):
                        q = 2 * hg + p
                        o3 = O32[:, 2 * p:2 * p + 2, :]
                        dve.wait_ge(co["ostd"], q + 1)
                        link(V.scalar_tensor_tensor(out=o3, in0=o3, scalar=col[:, C_GDNN:C_GDNN + 1],
                                                    in1=pairs(std[:, p, :]), op0=ALU.mult, op1=ALU.mult))
                        V.tensor_tensor(o3, o3, zs[:, 2 * q:2 * q + 2, :], ALU.mult).then_inc(co["onorm"], 1)
                    for p in range(2):
                        q = 2 * hg + p
                        dve.wait_ge(co["ohi"], q + 1)
                        V.tensor_tensor(hl[:, 2 * q:2 * q + 2, :], O32[:, 2 * p:2 * p + 2, :],
                                        hh[:, 2 * q:2 * q + 2, :].bitcast(F32), ALU.subtract).then_inc(co["olo"], 1)
                for n in range(PROJ_OUT - 1):
                    split_next(G_GDN_OUT + n, (G_GDN_OUT + n) % RAW)
                pool_columns(0, POOL_GDN, U_GDN)

            def angles():
                dve.wait_ge(consts_in, 48)
                C1 = 6.28125
                C2 = 0.0019350051879882812
                C3 = TWO_PI - C1 - C2
                link(V.tensor_copy(ang[:, 0, :], angi[:, :]))
                link(V.tensor_scalar(ang[:, 1, :], ang[:, 0, :], col[:, C_FREQ:C_FREQ + 1], None, ALU.mult))
                link(V.tensor_scalar(ang[:, 2, :], ang[:, 1, :], 1.0 / TWO_PI, RND, ALU.mult, ALU.add))
                link(V.tensor_scalar(ang[:, 3, :], ang[:, 2, :], RND, None, ALU.subtract))
                for c in (C1, C2, C3):
                    link(V.scalar_tensor_tensor(out=ang[:, 1, :], in0=ang[:, 3, :], scalar=-c, in1=ang[:, 1, :],
                                                op0=ALU.mult, op1=ALU.add))
                link(V.tensor_scalar(ang[:, 2, :], ang[:, 1, :], TWO_PI / 4, None, ALU.add))
                link(V.tensor_scalar(ang[:, 3, :], ang[:, 2, :], TWO_PI / 2, None, ALU.is_gt))
                link(V.scalar_tensor_tensor(out=ang[:, 2, :], in0=ang[:, 3, :], scalar=-TWO_PI, in1=ang[:, 2, :],
                                            op0=ALU.mult, op1=ALU.add))
                V.tensor_scalar(ang[:, 4, :], ang[:, 2, :], 3.1415925, -3.1415925, ALU.min, ALU.max)
                V.tensor_scalar(ang[:, 5, :], ang[:, 1, :], 3.1415925, -3.1415925, ALU.min, ALU.max).then_inc(am["angle"], 1)

            def sign_sin():
                dve.wait_ge(am["sin"], 1)
                V.tensor_scalar(cs[:, 1, :], cs[:, 1, :], col[:, C_SIGN:C_SIGN + 1], None, ALU.mult).then_inc(dve_link, 1)
                links[0] += 1

            def latent(nt, first):
                dve.wait_ge(am["latstd"], 1 if first else 2)
                link(V.reciprocal(rot[:, 0:T], std[:, 0, 0:T]))
                c0, i0 = (C_KVL, 0) if first else (C_QL, 2)
                for i in range(nt):
                    V.tensor_tensor(lat[:, i, :], lat[:, i, :], rot[:, 0:T], ALU.mult).then_inc(am["latn"], 1)
                for i in range(nt):
                    dve.wait_ge(am["lathi"], i0 + i + 1)
                    V.scalar_tensor_tensor(out=latl[:, i, :], in0=lat[:, i, :], scalar=col[:, c0 + i:c0 + i + 1],
                                           in1=lath[:, i, :].bitcast(F32), op0=ALU.mult, op1=ALU.subtract).then_inc(am["latlo"], 1)

            def rotary(src, n, c0):
                w = src.shape[1] // n
                for c in range(n):
                    part = src[:, c * w:(c + 1) * w, :]
                    tmp = rot[:, 0:w * T].rearrange("p (e t) -> p e t", e=w)
                    dve.wait_ge(am["swap"], c0 + c + 1)
                    V.tensor_tensor(tmp, swap_bank(n, c)[:, 0:w * T].rearrange("p (e t) -> p e t", e=w), wide(cs[:, 1, :], w), ALU.mult)
                    link(V.tensor_tensor(part, part, wide(cs[:, 0, :], w), ALU.mult))
                    link(V.tensor_tensor(part, part, tmp, ALU.add))

            def key_factors():
                dve.wait_ge(am["hss"], 4)
                link(V.tensor_copy(hst[:, 1, 0:2], bank[2][:, 2 * HEADS:2 * HEADS + 2]))
                V.tensor_tensor(hst[:, 0, :].rearrange("p (h b) -> p h b", b=2), bank[2][:, 0:2 * HEADS].rearrange("p (h b) -> p h b", b=2),
                                wide(hst[:, 1, 0:2], HEADS), ALU.add).then_inc(am["hsum"], 1)
                dve.wait_ge(am["hstd"], 1)
                link(V.reciprocal(hst[:, 2, :], hst[:, 1, :]))
                for j in range(4):
                    V.tensor_tensor(heads4(diagonal(j)), wide(mat[:, M_ID, :], 4),
                                    hst[:, 2, 4 * j:4 * j + 4].unsqueeze(2).to_broadcast([P, 4, P]), ALU.mult).then_inc(am["hdiag"], 1)

            def key_norm(j):
                dve.wait_ge(am["hcast"], j + 1)
                r = bank[4 + j]
                for e in range(2):
                    hp = slice(64 * e, 64 * e + 64)
                    V.tensor_tensor(kr[hp, j, :], lat[hp, 2, :], r[hp, e * T:(e + 1) * T], ALU.mult)
                V.scalar_tensor_tensor(out=kn[:, 2 * j:2 * j + 2, :], in0=kn[:, 2 * j:2 * j + 2, :], scalar=col[:, C_KN:C_KN + 1],
                                       in1=pairs(r[:, :]), op0=ALU.mult, op1=ALU.mult).then_inc(am["hn"], 1)

            def query_norms():
                dve.wait_ge(am["ropess"], 1)
                link(V.tensor_copy(hst[:, 1, :], bank[2][:, 2 * HEADS:4 * HEADS]))
                V.tensor_tensor(hst[:, 0, :], bank[2][:, 0:2 * HEADS], hst[:, 1, :], ALU.add).then_inc(am["hsum"], 1)
                dve.wait_ge(am["hstd"], 2)
                link(V.reciprocal(hst[:, 3, :], hst[:, 1, :]))

            def kv():
                g = G_KV
                split_next(g, g % RAW)
                latent(KV_LORA_T, True)
                split_next(g + 1, (g + 1) % RAW)
                dve.wait_ge(am["ropesq"], 1)
                V.tensor_scalar(lat[:, 2, :], lat[:, 2, :], col[:, C_KN + 1:C_KN + 2], None, ALU.mult).then_inc(am["gained"], 1)
                ada_step(U_KV, U_KV % 2)
                ada_step(U_KV + 1, (U_KV + 1) % 2)
                ada_step(U_KV + 2, (U_KV + 2) % 2)
                dve.wait_ge(am["gained"], 1)
                rotary(lat[:, 2:3, :], 1, 0)
                key_factors()
                split_next(g + 2, (g + 2) % RAW)

            def mla():
                g = G_MLA
                split_next(g, g % RAW)
                latent(Q_LORA_T, False)
                split_next(g + 1, (g + 1) % RAW)
                ada_finish(U_MLA)
                for p in range(3):
                    split_next(g + 2 + p, (g + 2 + p) % RAW)
                query_norms()
                rotary(qr[:, :, :], 2, 1)
                V.tensor_copy(st[:, 0, 4:5], hst[:, 3, 0:1]).then_inc(am["rotated"], 1)
                for i in range(HEADS + 4):
                    if i < HEADS:
                        e = i % 2
                        dve.wait_ge(am["s"], i + 1)
                        V.memset(bank[e][0:64, 64:128], NEG)
                        link(V.memset(bank[e][0:64, 448:512], NEG))
                        V.tensor_reduce(st[:, e, 0:1], bank[e][:, 0:P], AX, ALU.max, negate=True)
                        link(V.tensor_reduce(st[:, e, 1:2], bank[e][:, T:2 * T], AX, ALU.max, negate=True))
                        V.tensor_tensor(st[:, e, 6:8], st[:, e, 0:2], hst[:, 3, 2 * i:2 * i + 2], ALU.mult).then_inc(am["max"], 1)
                    if 1 <= i <= HEADS:
                        e = (i - 1) % 2
                        dve.wait_ge(am["exp"], i)
                        link(V.reciprocal(st[:, e, 4:6], st[:, e, 2:4]))
                        V.tensor_scalar(prb[:, e, 0:P], prb[:, e, 0:P], st[:, e, 4:5], None, ALU.mult)
                        V.tensor_scalar(prb[:, e, P:P + T], prb[:, e, P:P + T], st[:, e, 5:6], None, ALU.mult).then_inc(am["p"], 1)
                    if i >= 4:
                        dve.wait_ge(am["ohi"], i - 3)
                        V.tensor_tensor(hl[:, i - 4, :], half(6 + i % 2, 0), hh[:, i - 4, :].bitcast(F32),
                                        ALU.subtract).then_inc(am["olo"], 1)
                for n in range(PROJ_OUT - 1):
                    if n == 1:
                        pool_columns(POOL_GDN, POOL_MLA, U_MLA)
                    if n:
                        u = U_MLA + POOL_MLA + n - 1
                        ada_step(u, u % 2, finish=n > 1)
                    split_next(G_MLA_OUT + n, (G_MLA_OUT + n) % RAW)

            dve.wait_ge(c_ready, 1)
            ada_staged(0)
            angles()
            ada_staged(2)
            sign_sin()
            ada_staged(4)
            ada_staged(6)
            ada_staged(8)
            norm(0)
            split_lo(0, 0)
            dve.wait_ge(ada_cols, 1)
            four = lambda t: t[:, 0:2 * STAGED].rearrange("p (n c) -> p n c", c=4)[:, :, 2:4]
            link(V.tensor_tensor(four(mods), bank[2][:, T:T + STAGED].rearrange("p (n c) -> p n c", c=2), four(modb), ALU.add))
            gains(0, C_NORM)
            modulate(0, mod_index(0, 0))
            split_lo(1, 1)
            ada_step(STAGED, STAGED % 2, None, False)
            ffn(0)
            dve.wait_ge(ba_hi, 1)
            V.tensor_tensor(wbal[:, :, :], wba[:, :, :], wbah[:, :, :].bitcast(F32), ALU.subtract).then_inc(ba_lo, 1)
            residual("ffn0", mod_index(0, 2), 0.5, G_FFN[0] + 32)
            gains(mod_index(0, 3), C_NORM + 8)
            norm(1)
            modulate(1, mod_index(0, 3))
            split_next(G_GDN - 1, (G_GDN - 1) % RAW)
            gdn()
            residual("gdn", mod_index(0, 5), 1.0, G_GDN_OUT + 3)
            gains(mod_index(0, 6), C_NORM + 16)
            norm(2)
            modulate(2, mod_index(0, 6))
            split_next(G_FFN[1] - 1, (G_FFN[1] - 1) % RAW)
            ffn(1)
            residual("ffn1", mod_index(0, 8), 0.5, G_FFN[1] + 32)
            gains(9, C_KVN)
            norm(3)
            modulate(3, 9)
            split_next(G_KV - 1, (G_KV - 1) % RAW)
            kv()
            gains(mod_index(1, 0), C_NORM + 24)
            modulate(4, mod_index(1, 0))
            split_next(G_KV + 3, (G_KV + 3) % RAW)
            ffn(2)
            residual("ffn2", mod_index(1, 2), 0.5, G_FFN[2] + 32)
            gains(mod_index(1, 3), C_NORM + 32)
            norm(4)
            modulate(5, mod_index(1, 3))
            split_next(G_MLA - 1, (G_MLA - 1) % RAW)
            mla()
            residual("mla", mod_index(1, 5), 1.0, G_MLA_OUT + 3)
            ada_finish(U_FFN[3])
            gains(mod_index(1, 6), C_NORM + 40)
            norm(5)
            modulate(6, mod_index(1, 6))
            split_next(G_FFN[3] - 1, (G_FFN[3] - 1) % RAW)
            ffn(3)
            residual("ffn3", mod_index(1, 8), 0.5, G_FFN[3] + 32)

        @block.tensor
        def _(pe):
            M = nc.tensor.matmul
            skip = [BY_PE]

            def col_tile(dst, slot, i0, nk, src_h, src_l):
                for k in range(nk):
                    w = slice((i0 + k) * P, (i0 + k + 1) * P)
                    M(dst, wh[:, slot, w], src_h[:, k, :], start=k == 0, stop=False)
                    M(dst, wh[:, slot, w], src_l[:, k, :], start=False, stop=False)
                    ins = M(dst, wl[:, slot, w], src_h[:, k, :], start=False, stop=k == nk - 1)
                return ins

            def sum_unit():
                M(bank[3][:, 0:1], acc[:, 0:P], ones[:, 0:1], start=True, stop=True)
                M(bank[3][:, 1:2], acc[:, P:2 * P], ones[:, 0:1], start=True, stop=True).then_inc(ada_red, 1)

            def ada_reduce(u):
                pe.wait_ge(ada_mac, u * KD + (KD - skip[0] * KD))
                pe.wait_ge(ada_done, u - skip[0])
                sum_unit()

            def pair_part(b, slot, k):
                for e in range(2):
                    w = slice((e * KD + k) * P, (e * KD + k + 1) * P)
                    M(half(b, e), wh[:, slot, w], hh[:, k, :], start=k == 0 and e == 0, stop=False, skip_group_check=True)
                    M(half(b, e), wh[:, slot, w], hl[:, k, :], start=False, stop=False, skip_group_check=True)
                    ins = M(half(b, e), wl[:, slot, w], hh[:, k, :], start=False, stop=k == KD - 1, skip_group_check=True)
                return ins

            def first_pair(b, slot, n):
                for k in range(KD):
                    pe.wait_ge(h_ready, 8 * n + k + 1)
                    ins = pair_part(b, slot, k)
                return ins

            def pool_reduce(n, c):
                pe.wait_ge(ada_pool, n + 1)
                M(bank[3][:, 2 * c:2 * c + 1], pacc[:, n % 4, 0:P], ones[:, 0:1], start=True, stop=True)
                M(bank[3][:, 2 * c + 1:2 * c + 2], pacc[:, n % 4, P:2 * P], ones[:, 0:1], start=True, stop=True).then_inc(pool_red, 1)

            def prologue_units():
                stats(0)
                pe.wait_ge(c_ready, 1)
                for n in range(BY_PE):
                    u = 2 * n + 1
                    pe.wait_ge(ada_mac, (n + 1) * KD)
                    if n:
                        pe.wait_ge(ada_done, n)
                    sum_unit()
                    pe.wait_ge(staged[u], 16)
                    for k in range(KD):
                        ins = M(bank[n // 2][0:1, n % 2 * T:n % 2 * T + T], cact[:, k:k + 1], staged_unit(u)[:, k, :],
                                start=k == 0, stop=k == KD - 1)
                ins.then_inc(pe_units, 1)
                pe.wait_ge(ada_rows, 1)
                for c in range(2 * BY_PE):
                    ins = M(bank[2][:, T + c:T + c + 1], arow[0:1, c * P:c * P + P], ones[0:1, 0:1], start=True, stop=True)
                ins.then_inc(ada_cols, 1)

            def stats(v, m0=0, m1=KD):
                for m in range(m0, m1):
                    pe.wait_ge(sq_ready, 8 * v + m + 1)
                    M(half(2, 0), mean_d[:, :], sq[:, m // 2 % 2, m % 2 * T:m % 2 * T + T], start=m == 0, stop=m == KD - 1).then_inc(ss_mm, 1)

            def ffn_in_step(f, g, j, slot, par, n=None, unit=None):
                pe.wait_ge(w_lo, g + 1)
                if not (isinstance(j, int) and 22 * f + j < 2):
                    pe.wait_ge(ff_hid, j + (22 * f - 1))
                if n is None:
                    col_tile(half(par, 0), slot, 0, KD, hh, hl)
                    col_tile(half(par, 1), slot, KD, KD, hh, hl).then_inc(w_used, 1)
                else:
                    first_pair(par, slot, n).then_inc(w_used, 1)
                if unit is not None:
                    ada_reduce(unit)

            def out_step(g, slot, kt, src_h, src_l, first=False, last=False, unit=None, stats_v=None):
                for m in range(KD):
                    dst = half(4 + m // 2, m % 2)
                    for k in range(2):
                        w = slice((k * KD + m) * P, (k * KD + m + 1) * P)
                        M(dst, wh[:, slot, w], src_h[:, kt + k, :], start=first and k == 0 and m % 2 == 0, stop=False,
                          skip_group_check=True)
                        M(dst, wh[:, slot, w], src_l[:, kt + k, :], start=False, stop=False, skip_group_check=True)
                        ins = M(dst, wl[:, slot, w], src_h[:, kt + k, :], start=False, stop=last and k == 1,
                                skip_group_check=True)
                    if last and m % 2 and m < KD - 1:
                        ins.then_inc(y_done, 1)
                    if m == KD - 1:
                        ins.then_inc(w_used, 1)
                    if last and stats_v < norms and m >= 5 and m % 2:
                        stats(stats_v, m - 5, m - 3)
                if unit is not None:
                    ada_reduce(unit)

            def ffn(f, n, v):
                g0, u0, last = G_FFN[f], U_FFN[f], f == 3
                for j in (0, 1):
                    unit = u0 - 1 if j == 0 and f == 0 else None
                    ffn_in_step(f, g0 + j, j, (g0 + j) % 2, j, n if j == 0 else None, unit)
                    if f == 2 and j == 0:
                        pe.wait_ge(am["vev"], 4)
                        for h in range(4):
                            pe.wait_ge(am["hdiag"], h + 1)
                            M(bank[4 + h][:, :], ones[:, :], diagonal(h), start=True, stop=True).then_inc(am["hcast"], 1)
                with pe.Fori(0, 5) as i:
                    for q in range(4):
                        unit = i * 2 + (u0 + q // 2) if not last and q % 2 == 0 else None
                        ffn_in_step(f, i * 4 + (g0 + 2 + q), i * 4 + (2 + q), (g0 + 2 + q) % 2, q % 2, unit=unit)
                g1 = g0 + FFN_IN
                turns = 1 if last else 2
                u1 = u0 + 1 if last else u0 + 11

                def step(o, g, slot, unit, **kw):
                    pe.wait_ge(w_lo, g + 1)
                    pe.wait_ge(ff_lo, o * 2 + (22 * f + 2))
                    out_step(g, slot, o * 2, fh, fl, unit=unit, **kw)

                step(0, g1, g1 % 2, None, first=True)
                with pe.Fori(0, turns) as i:
                    for q in range(4):
                        step(i * 4 + (1 + q), i * 4 + (g1 + 1 + q), (g1 + 1 + q) % 2,
                             i * 2 + (u1 - 1 + q // 2) if q % 2 == 0 else None)
                u2, o1 = u1 + 2 * turns, 1 + 4 * turns
                for o in range(o1, FFN_OUT):
                    unit = u2 - 1 if o == o1 else u2 if last and o == o1 + 2 else None
                    step(o, g1 + o, (g1 + o) % 2, unit, last=o == FFN_OUT - 1, stats_v=v)

            def project(g0, ready, count, v, after=None):
                pe.wait_ge(ready, count)
                for n in range(PROJ_OUT):
                    g = g0 + n
                    pe.wait_ge(w_lo, g + 1)
                    out_step(g, g % 2, 2 * n, hh, hl, first=n == 0, last=n == PROJ_OUT - 1, stats_v=v)
                    if after is not None:
                        after(n)

            def gdn(n):
                pe.wait_ge(ba_lo, 1)
                for k in range(KD):
                    pe.wait_ge(h_ready, 8 * n + k + 1)
                    dst = bank[2][0:16, 0:T]
                    M(dst, wbah[:, k, :], hh[:, k, :], start=k == 0, stop=False)
                    M(dst, wbah[:, k, :], hl[:, k, :], start=False, stop=False)
                    ba = M(dst, wbal[:, k, :], hh[:, k, :], start=False, stop=k == KD - 1)
                    if k == KD - 1:
                        ba.then_inc(ba_done, 1)
                    if k == 0:
                        pe.wait_ge(w_lo, G_GDN + 1)
                    ins = pair_part(0, G_GDN % 2, k)
                ins.then_inc(w_used, 1)
                ada_reduce(U_GDN - 1)

                def tile_pair(g, slot, par, free, unit):
                    pe.wait_ge(w_lo, g + 1)
                    if free is not None:
                        pe.wait_ge(*free)
                    col_tile(half(par, 0), slot, 0, KD, hh, hl)
                    col_tile(half(par, 1), slot, KD, KD, hh, hl).then_inc(w_used, 1)
                    if unit is not None:
                        ada_reduce(unit)

                for m in range(1, 4):
                    g = G_GDN + m
                    tile_pair(g, g % 2, m % 2, (gc_conv, 2 * m - 2) if m > 1 else None, None)
                    if m == 1:
                        pe.wait_ge(ba_sb, 1)
                        for b in range(2):
                            ins = nc.tensor.transpose(bank[2][:, T + 16 * b:T + 16 * b + 16], bas[:, b * P:b * P + P], mat[0:16, M_ID, 0:16])
                        ins.then_inc(ba_turned, 1)
                    if m == 3:
                        pe.wait_ge(ada_done, U_GDN - BY_PE)
                        pool_reduce(0, 0)
                with pe.Fori(0, 2) as i:
                    for m in range(4, 8):
                        g = G_GDN + m
                        tile_pair(i * 4 + g, g % 2, m % 2, (gc_conv, i * 8 + (2 * m - 2)), None)
                for m in range(12, 16):
                    g = G_GDN + m
                    tile_pair(g, g % 2, m % 2, (gc_conv, 2 * m - 2) if m < 14 else (gz_silu, m - 13), None)
                    pool_reduce(m - 11, m - 11)
                    p = m - 12
                    pe.wait_ge(l2_sq, p + 1)
                    for h in range(2):
                        for b in range(2):
                            c = 64 + 8 * b + 2 * p + h
                            ins = M(bank[2][:, c:c + 1], sq[:, p % 2, h * T + b * P:h * T + b * P + P], ones[:, 0:1], start=True, stop=True)
                    ins.then_inc(l2_ss, 1)
                pe.wait_ge(gt_dve, 2)
                for b in range(2):
                    M(bank[2][:, 32 + 8 * b:40 + 8 * b], mat[:, M_LE, :], sc[:, 1, b, :], start=True, stop=True)
                    ins = M(bank[2][:, 48 + 8 * b:56 + 8 * b], mat[:, M_GT, :], sc[:, 1, b, :], start=True, stop=True)
                ins.then_inc(gt_pe, 1)
                pe.wait_ge(gz_silu, 4)
                for hg in range(2):
                    def kq(which, h, b):
                        return qkv[:, 8 * which + 4 * hg + h, b * P:b * P + P]

                    def cols4(h):
                        return slice(P * h, P * h + P)

                    for b in range(2):
                        s = 2 * hg + b
                        if hg:
                            pe.wait_ge(co["ostd"] if b else co["osb"], 2)
                        for h in range(4):
                            M(bank[b][:, cols4(h)], kq(1, h, b), kq(1, h, b), start=True, stop=True)
                        for h in range(4):
                            M(bank[4 + b][:, cols4(h)], kq(1, h, b), kq(0, h, b), start=True, stop=True)
                        pe.wait_ge(co["gm"], s + 1)
                        M(bank[6 + b][:, :], ones[:, :], TMP[:, 0, :], start=True, stop=True).then_inc(co["gq"], 1)
                        pe.wait_ge(co["bm"], s + 1)
                        if s:
                            pe.wait_ge(co["bs"], s)
                        M(bank[2][:, :], ones[:, :], TMP[:, 1, :], start=True, stop=True).then_inc(co["kq"], 1)
                    for b in range(2):
                        s = 2 * hg + b
                        pe.wait_ge(co["lt"], s + 1)
                        for h in range(4):
                            ins = nc.tensor.transpose(bank[b][:, cols4(h)], LT[:, b, cols4(h)], mat[:, M_ID, :])
                        ins.then_inc(co["turned"], 1)
                        pe.wait_ge(co["at"], s + 1)
                        for h in range(4):
                            nc.tensor.transpose(bank[4 + b][:, cols4(h)], kq(1, h, b), mat[:, M_ID, :])
                        for h in range(4):
                            ins = nc.tensor.transpose(bank[6 + b][:, cols4(h)], kq(2, h, b), mat[:, M_ID, :])
                        ins.then_inc(co["kvt"], 1)

                    if hg:
                        pool_reduce(POOL_GDN - 3, POOL_GDN - 3)
                    pe.wait_ge(co["tokd"], 2 * hg + 2)
                    with pe.Fori(1, LEVELS - 1) as lv:
                        for b in range(2):
                            pe.wait_ge(inv_x[b], lv + 7 * hg)
                            for h in range(4):
                                ins = M(bank[b][:, cols4(h)], LT[:, b, cols4(h)], X[:, b, cols4(h)], start=True, stop=True)
                            ins.then_inc(inv_p[b], 1)
                        for b in range(2):
                            pe.wait_ge(inv_ps[b], lv + 6 * hg)
                            for h in range(4):
                                M(bank[4 + b][:, cols4(h)], XT[:, b, cols4(h)], PS[:, b, cols4(h)], start=True, stop=True)
                            for h in range(4):
                                ins = M(bank[6 + b][:, cols4(h)], PS[:, b, cols4(h)], XT[:, b, cols4(h)], start=True, stop=True)
                            ins.then_inc(inv_xp[b], 1)
                    for b in range(2):
                        pe.wait_ge(inv_x[b], 6 + 7 * hg)
                        for h in range(4):
                            ins = M(bank[b][:, cols4(h)], LT[:, b, cols4(h)], X[:, b, cols4(h)], start=True, stop=True)
                        ins.then_inc(inv_p[b], 1)
                    for b in range(2):
                        pe.wait_ge(inv_ps[b], 6 + 6 * hg)
                        for h in range(4):
                            ins = M(bank[6 + b][:, cols4(h)], PS[:, b, cols4(h)], XT[:, b, cols4(h)], start=True, stop=True)
                        ins.then_inc(inv_xp[b], 1)
                    for b in range(2):
                        s = 2 * hg + b
                        pe.wait_ge(inv_x[b], 7 + 7 * hg)
                        if b:
                            for h in range(4):
                                M(bank[4 + b][:, cols4(h)], RK[:, cols4(h)], XT[:, b, cols4(h)], start=True, stop=True)
                        for h in range(4):
                            ins = M(bank[b][:, cols4(h)], XT[:, b, cols4(h)], RV[:, b, cols4(h)], start=True, stop=True)
                        ins.then_inc(co["u"], 1)
                    pool_reduce(POOL_GDN - 5 + 3 * hg, POOL_GDN - 5 + 3 * hg)
                    pe.wait_ge(co["uu"], 2 * hg + 1)
                    for h in range(4):
                        ins = M(bank[6][:, cols4(h)], KDC[:, cols4(h)], U[:, 0, cols4(h)], start=True, stop=True)
                    ins.then_inc(co["state"], 1)
                    for h in range(4):
                        ins = M(bank[4][:, cols4(h)], U[:, 0, cols4(h)], AT[:, 0, cols4(h)], start=True, stop=True)
                    ins.then_inc(co["o0"], 1)
                    pe.wait_ge(co["state_sb"], hg + 1)
                    pe.wait_ge(co["uu"], 2 * hg + 2)
                    for h in range(4):
                        ins = M(bank[7][:, cols4(h)], WT[:, cols4(h)], SS[:, cols4(h)], start=True, stop=True)
                    ins.then_inc(co["ws"], 1)
                    pe.wait_ge(co["vnew"], hg + 1)
                    for h in range(4):
                        M(bank[1][:, cols4(h)], SS[:, cols4(h)], QG[:, cols4(h)], start=True, stop=False)
                        ins = M(bank[1][:, cols4(h)], U[:, 1, cols4(h)], AT[:, 1, cols4(h)], start=False, stop=True)
                    ins.then_inc(co["o1"], 1)
                    pe.wait_ge(co["qsq"], hg + 1)
                    for p in range(2):
                        M(bank[5 + 2 * p][:, :], eps_hd[:, :], TMP[:, p, :], start=True, stop=False)
                    for p in range(2):
                        pe.wait_ge(co["osq"], 2 * hg + p + 1)
                        M(bank[5 + 2 * p][:, :], mean_hd[:, :], sq[:, p, :], start=False, stop=True).then_inc(co["oss"], 1)
                    pool_reduce(POOL_GDN - 4 + 3 * hg, POOL_GDN - 4 + 3 * hg)
                project(G_GDN_OUT, co["olo"], 4, 2)
                skip[0] += POOL_GDN

            def latent_sum(nt, count):
                pe.wait_ge(am["latsq"], count)
                M(half(2, 0), ones[:, :], sq[:, 0, 0:T], start=True, stop=False)
                ins = M(half(2, 0), ones[:, :], sq[:, 0, T:2 * T], start=False, stop=nt == 2)
                if nt == 3:
                    ins = M(half(2, 0), ones[:, :], sq[:, 1, 0:T], start=False, stop=True)
                ins.then_inc(am["latss"], 1)

            def swaps(src, n, c0):
                w = src.shape[1] // n
                for c in range(n):
                    M(swap_bank(n, c)[:, 0:w * T], mat[:, M_SWAP, :], src[:, c * w:(c + 1) * w, :], start=True, stop=True).then_inc(am["swap"], 1)

            def head_sums(p, n):
                pe.wait_ge(am["hsq"], n + 1)
                for e in range(2):
                    for b in range(2):
                        c = 4 * p + 2 * e + b
                        ins = M(bank[2][:, c:c + 1], sq[:, p % 2, e * T + b * P:e * T + b * P + P], ones[:, 0:1], start=True, stop=True)
                ins.then_inc(am["hss"], 1)

            def kv(n):
                g = G_KV
                pe.wait_ge(w_lo, g + 1)
                first_pair(0, g % 2, n).then_inc(w_used, 1)
                ada_reduce(U_KV - 1)
                pe.wait_ge(w_lo, g + 2)
                col_tile(half(1, 0), (g + 1) % 2, 0, KD, hh, hl).then_inc(w_used, 1)
                latent_sum(KV_LORA_T, 1)
                pe.wait_ge(w_lo, g + 3)
                pe.wait_ge(am["latlo"], 2)
                pe.wait_ge(am["ropesq"], 1)
                for b in range(2):
                    c = 2 * HEADS + b
                    M(bank[2][:, c:c + 1], sqr[:, 0, b * P:b * P + P], mat[:, M_LOW, 0:1], start=True, stop=True)
                for p in range(4):
                    if p >= 2:
                        pe.wait_ge(am["hsq"], p - 1)
                    for e in range(2):
                        ins = col_tile(half(p % 2, e), g % 2, 2 * (2 * p + e), 2, lath, latl)
                    ins.then_inc(am["kraw"] if p < 3 else w_used, 1)
                    if p:
                        head_sums(p - 1, p - 1)
                    if p == 1:
                        ada_reduce(U_KV)
                head_sums(3, 3)
                ada_reduce(U_KV + 1)
                pe.wait_ge(am["gained"], 1)
                swaps(lat[:, 2:3, :], 1, 0)
                pe.wait_ge(w_lo, g + 4)
                for b in range(2):
                    for c in range(2):
                        dst = bank[4 + 2 * b + c][:, :]
                        for k in range(2):
                            ht = slice(b * P, b * P + P)
                            w = slice(D * k + 512 * c, D * k + 512 * c + 512)
                            sl = (g + 3) % 2
                            M(dst, lath[:, k, ht], wh[:, sl, w], start=k == 0, stop=False)
                            M(dst, latl[:, k, ht], wh[:, sl, w], start=False, stop=False)
                            ins = M(dst, lath[:, k, ht], wl[:, sl, w], start=False, stop=k == 1)
                ins.then_inc(w_used, 1)

            def mla(n):
                g = G_MLA
                pe.wait_ge(w_lo, g + 1)
                first_pair(0, g % 2, n).then_inc(w_used, 1)
                ada_reduce(U_MLA - 1)
                pe.wait_ge(w_lo, g + 2)
                col_tile(half(1, 0), (g + 1) % 2, 0, KD, hh, hl).then_inc(w_used, 1)
                latent_sum(Q_LORA_T, 3)
                for p in range(6):
                    if p % 2 == 0:
                        pe.wait_ge(w_lo, g + 2 + p // 2 + 1)
                    if p == 0:
                        pe.wait_ge(am["latlo"], 5)
                    if p >= 2:
                        pe.wait_ge(am["hsq"], p + 3)
                    for e in range(2):
                        ins = col_tile(half(p % 2, e), (g + 2 + p // 2) % 2, 3 * (2 * (p % 2) + e), 3, lath, latl)
                    ins.then_inc(w_used if p % 2 else am["qraw"], 1)
                    if 1 <= p <= 4:
                        head_sums(p - 1, p + 3)
                pe.wait_ge(ada_done, U_MLA - skip[0])
                pool_reduce(POOL_GDN, 0)
                pool_reduce(POOL_GDN + 1, 1)
                pe.wait_ge(am["ropesq"], 3)
                swaps(qr[:, :, :], 2, 1)
                for j in range(4):
                    for b in range(2):
                        c = 2 * HEADS + 4 * j + b
                        ins = M(bank[2][:, c:c + 3:2], sqr[:, j, b * P:b * P + P], mat[:, M_LOW:M_HIGH + 1, 0], start=True, stop=True)
                ins.then_inc(am["ropess"], 1)
                pe.wait_ge(am["rotated"], 1)
                for i in range(HEADS + 3):
                    if i < HEADS:
                        h, e, j = i, i % 2, i // 2
                        hp = slice(64 * (h % 2), 64 * (h % 2) + 64)
                        if h >= 2:
                            pe.wait_ge(am["exp"], h - 1)
                        for qb in range(2):
                            qs = slice(qb * P, qb * P + P)
                            dst = bank[e][:, qb * T:qb * T + P * (qb + 1)]
                            M(dst, qn[:, h, qs], kn[:, h, 0:P * (qb + 1)], start=True, stop=False)
                            ins = M(dst, qr[hp, j, qs], kr[hp, j, 0:P * (qb + 1)], start=False, stop=True)
                        ins.then_inc(am["s"], 1)
                    if 2 <= i < HEADS + 2:
                        h = i - 2
                        pe.wait_ge(am["p"], h + 1)
                        if h >= 2:
                            pe.wait_ge(am["pt"], h - 1)
                        for c in range(3):
                            ins = nc.tensor.transpose(bank[4 + h % 2][:, P * c:P * c + P], prb[:, h % 2, P * c:P * c + P], mat[:, M_ID, :])
                        ins.then_inc(am["turned"], 1)
                    if i >= 3:
                        h = i - 3
                        pe.wait_ge(am["pt"], h + 1)
                        if h >= 2:
                            pe.wait_ge(am["olo"], h - 1)
                        v = [vt[:, b, P * h:P * h + P] for b in range(2)]
                        dst = bank[6 + h % 2]
                        M(dst[:, 0:P], v[0], pt[:, h % 2, 0:P], start=True, stop=True)
                        M(dst[:, P:2 * P], v[0], pt[:, h % 2, P:2 * P], start=True, stop=False)
                        M(dst[:, P:2 * P], v[1], pt[:, h % 2, 2 * P:3 * P], start=False, stop=True).then_inc(am["o"], 1)
                    if i in (2, 6):
                        pool_reduce(POOL_GDN + 2 + i // 4, 2 + i // 4)

                def sums(n):
                    if n == 0:
                        pool_reduce(POOL_GDN + POOL_MLA - 1, POOL_MLA - 1)
                        skip[0] += POOL_MLA
                    if n in (1, 2):
                        ada_reduce(U_MLA + POOL_MLA + n - 1)

                project(G_MLA_OUT, am["olo"], HEADS, 5, sums)

            pe.wait_ge(set_consts, 1)
            prologue_units()
            ffn(0, 0, 1)
            stats(1, KD // 2)
            gdn(1)
            stats(2, KD // 2)
            ffn(1, 2, 3)
            stats(3, KD // 2)
            kv(3)
            ffn(2, 4, 4)
            stats(4, KD // 2)
            mla(5)
            stats(5, KD // 2)
            ffn(3, 6, 6)


def square_consts():
    import numpy as np
    i = np.arange(P)
    out = np.zeros((P, M_COUNT, P), np.float32)
    row, colm = i[:, None], i[None, :]
    out[:, M_ID] = row == colm
    out[:, M_LE] = row <= colm
    out[:, M_GT] = row > colm
    out[:, M_ST] = row < colm
    out[:, M_SWAP] = row == (colm ^ 32)
    out[:, M_LOW] = row + 0 * colm < P // 2
    out[:, M_HIGH] = row + 0 * colm >= P // 2
    for lv in range(LEVELS):
        s = 1 << lv
        low = (row // (2 * s) == colm // (2 * s)) & (row // s % 2 == 1) & (colm // s % 2 == 0)
        out[:, M_LV + lv] = low
        if lv == 0:
            out[:, M_LVT] = low.T
    return out


def kernel(**inputs):
    import numpy as np
    import concourse.bacc as bacc
    from concourse.bass_utils import run_bass_kernel_spmd

    a = {k: np.asarray(v) for k, v in inputs.items()}
    f32 = np.float32

    def by_partition(v):
        v = v.reshape(v.shape[:-1] + (v.shape[-1] // P, P))
        return np.moveaxis(v, -1, 0).reshape(P, -1)

    def tiles(w):
        return w.reshape(w.shape[0] // P, P, w.shape[1] // P, P).transpose(2, 0, 1, 3)

    def granule(t, per=TILES):
        g = np.zeros((len(t) // per, P, TILES, P), f32)
        g[:, :, :per] = t.reshape(-1, per, P, P).transpose(0, 2, 1, 3)
        return g.reshape(-1, P, GW)

    def ffn(l, i):
        w = tiles(a["ffn_w_in"][l, i])
        both = np.stack([w[:FT], w[FT:]], 1)
        o = tiles(a["ffn_w_out"][l, i]).transpose(1, 0, 2, 3)
        return [granule(both.reshape(-1, P, P)), granule(o.reshape(-1, P, P))]

    def proj(w):
        return granule(tiles(w).transpose(1, 0, 2, 3).reshape(-1, P, P))

    gin = a["gdn_w_in"][0]
    dkv = a["mla_w_dkv"]
    rope = tiles(np.concatenate([dkv[:, 256:], dkv[:, 256:]], 1))[0]
    ukv = a["mla_w_ukv"].reshape(256, HEADS, 256)
    uv = ukv[:, :, P:].reshape(2, P, D).transpose(1, 0, 2).reshape(1, P, GW)
    uq = a["mla_w_uq"][0].reshape(Q_LORA_T * P, HEADS, QK_HEAD)
    uq_all = np.concatenate([uq[:, :, :P].reshape(-1, D), uq[:, :, P:].reshape(-1, D // 2)], 1)
    dq = tiles(a["mla_w_dq"][0])
    wstream = np.concatenate(
        ffn(0, 0) + [granule(tiles(gin[:, :4 * D]).reshape(-1, P, P)), proj(a["gdn_w_out"][0])] + ffn(0, 1)
        + [granule(tiles(dkv[:, :256]).reshape(-1, P, P)), granule(rope, KD),
           granule(tiles(np.ascontiguousarray(ukv[:, :, :P]).reshape(256, D)).reshape(-1, P, P)), uv] + ffn(1, 0)
        + [granule(dq[:2].reshape(-1, P, P)), granule(dq[2], KD), granule(tiles(uq_all).reshape(-1, P, P), 12),
           proj(a["mla_w_out"][0])] + ffn(1, 1))
    assert wstream.shape[0] == GRANULES

    def ada_units(w):
        return w.reshape(KD, P, -1, 256).transpose(2, 1, 0, 3)

    ada = np.concatenate([ada_units(a["ada_w"][0]), ada_units(a["kv_ada_w"]), ada_units(a["ada_w"][1])])
    ada_b = np.concatenate([by_partition(a["ada_b"][0]), by_partition(a["kv_ada_b"]), by_partition(a["ada_b"][1])], 1)
    half = 32
    freq = (f32(10000.0) ** (-np.arange(half, dtype=f32) / f32(half))).astype(f32)
    kg, qg = a["mla_k_norm_g"], a["mla_q_norm_g"][0]
    cols = np.zeros((P, C_COLS), f32)
    cols[:, C_NORM:C_NORM + 48] = by_partition(a["norm_g"])
    cols[:, C_KVN:C_KVN + 8] = by_partition(a["kv_norm_g"])
    cols[:, C_CONV:C_CONV + 96] = by_partition(a["gdn_conv_w"][0])
    cols[:, C_GDNN] = a["gdn_norm_g"][0]
    cols[:, C_KVL:C_KVL + 2] = by_partition(a["mla_kv_norm_g"])
    cols[:, C_QL:C_QL + 3] = by_partition(a["mla_q_lora_norm_g"])
    cols[:, C_KN], cols[:, C_KN + 1] = kg[:P], np.tile(kg[P:], 2)
    cols[:, C_QN], cols[:, C_QN + 1] = qg[:P], np.tile(qg[P:], 2)
    cols[:, C_FREQ] = np.tile(freq, 4)
    cols[:, C_SIGN] = np.tile(np.repeat(np.array([-1.0, 1.0], f32), half), 2)
    tok = np.broadcast_to(np.concatenate([a["gdn_dt_bias"][0], a["gdn_a_log"][0]]), (P, 16))
    arrays = {
        "x_in": a["x"][0].T.reshape(KD, P, T).transpose(1, 0, 2),
        "c_in": by_partition(a["c"][0]),
        "pos_in": np.broadcast_to(a["positions"][0], (P, T)),
        "wstream": wstream, "ada": ada, "ada_b": ada_b, "cols": cols, "tok": tok,
        "wba": gin[:, 4 * D:].reshape(KD, P, 16).transpose(1, 0, 2),
        "squares": square_consts(),
    }
    arrays = {k: np.ascontiguousarray(v) for k, v in arrays.items()}
    nc = bacc.Bacc("TRN2", target_bir_lowering=False, num_devices=1)
    args = [nc.dram_tensor(k, v.shape, mybir.dt.from_np(v.dtype), kind="ExternalInput").ap() for k, v in arrays.items()]
    args.append(nc.dram_tensor("y_out", (P, KD, T), F32, kind="ExternalOutput").ap())
    build(nc, *args)
    r = run_bass_kernel_spmd(nc, [arrays], core_ids=[0])
    y = r.results[0]["y_out"]
    return y.transpose(1, 0, 2).reshape(1, D, T).transpose(0, 2, 1)
```
